# Optimizing a Trainium2 kernel written in Bass

```python
import jax, jax.numpy as jnp
from jax import lax
import numpy as np

D_MODEL = 2048
BATCH = 1
SEQ = 1024
DEPTH = 1
DEC_BATCH = 1
DEC_SEQ = 64
PAST_LEN = 256

CHUNK = 64
E_POOL = 1024
N_POOL_GROUPS = 4
POOL_GROUP = E_POOL // N_POOL_GROUPS
POOL_WINDOWS = (2, 4, 8, 16)
POOL_BUF = max(POOL_WINDOWS) - 1
E_CONV = 1024
CONV_WIDTH = 3
CONV_BUF = CONV_WIDTH - 1
SPLIT_SIZES = (E_POOL, E_POOL, E_CONV, E_CONV, E_CONV, E_CONV, D_MODEL, D_MODEL)
IN_COLS = sum(SPLIT_SIZES)
SPLIT_IDX = tuple(int(i) for i in np.cumsum(SPLIT_SIZES)[:-1])
EPS = 1e-6

kernel_name = 'hybrid_pool_shortconv_gated_stream_step'

def rmsnorm(x, g):
    xf = x.astype(jnp.float32)
    r = lax.rsqrt(jnp.mean(xf * xf, axis=-1, keepdims=True) + EPS)
    return (xf * r * g.astype(jnp.float32)).astype(x.dtype)

def pool_mixer(xa, buf, offset, w_mix, scale):
    B, T, _ = xa.shape
    xp = jnp.concatenate([buf.astype(xa.dtype), xa], axis=1).astype(jnp.float32)
    cs = jnp.pad(jnp.cumsum(xp, axis=1), ((0, 0), (1, 0), (0, 0)))
    pos = offset + jnp.arange(T, dtype=jnp.int32)
    outs = []
    for g, w in enumerate(POOL_WINDOWS):
        sl = slice(g * POOL_GROUP, (g + 1) * POOL_GROUP)
        s = cs[:, POOL_BUF + 1:POOL_BUF + 1 + T, sl] - cs[:, POOL_BUF + 1 - w:POOL_BUF + 1 - w + T, sl]
        cnt = jnp.minimum(pos + 1, w).astype(jnp.float32)[None, :, None]
        outs.append(s / cnt - xp[:, POOL_BUF:, sl])
    d = jnp.stack(outs, axis=2)
    mixed = jnp.einsum('btgc,gcd->btgd', d, w_mix.astype(jnp.float32))
    y = mixed.reshape(B, T, E_POOL) * scale.astype(jnp.float32)
    return y.astype(xa.dtype), xp[:, -POOL_BUF:].astype(xa.dtype)

def conv_mixer(u, buf, w_conv):
    T = u.shape[1]
    up = jnp.concatenate([buf.astype(u.dtype), u], axis=1)
    y = w_conv[0] * up[:, 0:T] + w_conv[1] * up[:, 1:1 + T] + w_conv[2] * up[:, 2:2 + T]
    return y, up[:, -CONV_BUF:]

def layer(x, pool_buf, conv_buf, offset, norm_g, w_in, b_gate, w_pool_mix, pool_scale,
          w_conv, w_proj_pool, w_proj_conv, w_out):
    h = rmsnorm(x, norm_g)
    proj = jnp.einsum('btd,dc->btc', h, w_in)
    xa, za, v, bg, cg, zb, ga, gb = jnp.split(proj, SPLIT_IDX, axis=-1)
    ya, new_pool = pool_mixer(xa, pool_buf, offset, w_pool_mix, pool_scale)
    ya = ya * jax.nn.silu(za)
    yc, new_conv = conv_mixer(cg * v, conv_buf, w_conv)
    yb = bg * yc * jax.nn.silu(zb)
    merged = (jax.nn.sigmoid(ga + b_gate[:D_MODEL]) * jnp.einsum('bte,ed->btd', ya, w_proj_pool)
              + jax.nn.sigmoid(gb + b_gate[D_MODEL:]) * jnp.einsum('bte,ed->btd', yb, w_proj_conv))
    x = x + jnp.einsum('btd,de->bte', merged, w_out)
    return x, new_pool, new_conv

def trunk(x, pool_bufs, conv_bufs, offset, norm_g, w_in, b_gate, w_pool_mix, pool_scale,
          w_conv, w_proj_pool, w_proj_conv, w_out, final_norm_g):
    new_pools, new_convs = [], []
    for l in range(DEPTH):
        x, npool, nconv = layer(x, pool_bufs[l], conv_bufs[l], offset, norm_g[l], w_in[l], b_gate[l],
                                w_pool_mix[l], pool_scale[l], w_conv[l], w_proj_pool[l],
                                w_proj_conv[l], w_out[l])
        new_pools.append(npool)
        new_convs.append(nconv)
    return rmsnorm(x, final_norm_g), jnp.stack(new_pools, axis=0), jnp.stack(new_convs, axis=0)

def setup_inputs(seed: int = 0) -> dict:
    key = jax.random.key(seed)
    ks = jax.random.split(key, 14)
    f32 = jnp.float32
    return {
        'x_prompt': jax.random.normal(ks[0], (BATCH, SEQ, D_MODEL), f32),
        'x_sample': jax.random.normal(ks[1], (DEC_BATCH, DEC_SEQ, D_MODEL), f32),
        'state_pool': jax.random.normal(ks[2], (DEPTH, DEC_BATCH, POOL_BUF, E_POOL), f32),
        'state_conv': jax.random.normal(ks[3], (DEPTH, DEC_BATCH, CONV_BUF, E_CONV), f32),
        'norm_g': 1.0 + 0.02 * jax.random.normal(ks[4], (DEPTH, D_MODEL), f32),
        'w_in': jax.random.normal(ks[5], (DEPTH, D_MODEL, IN_COLS), f32) * D_MODEL ** -0.5,
        'b_gate': 0.02 * jax.random.normal(ks[6], (DEPTH, 2 * D_MODEL), f32),
        'w_pool_mix': jax.random.normal(ks[7], (DEPTH, N_POOL_GROUPS, POOL_GROUP, POOL_GROUP), f32) * POOL_GROUP ** -0.5,
        'pool_scale': 1.0 + 0.02 * jax.random.normal(ks[8], (DEPTH, E_POOL), f32),
        'w_conv': jax.random.normal(ks[9], (DEPTH, CONV_WIDTH, E_CONV), f32) * CONV_WIDTH ** -0.5,
        'w_proj_pool': jax.random.normal(ks[10], (DEPTH, E_POOL, D_MODEL), f32) * E_POOL ** -0.5,
        'w_proj_conv': jax.random.normal(ks[11], (DEPTH, E_CONV, D_MODEL), f32) * E_CONV ** -0.5,
        'w_out': jax.random.normal(ks[12], (DEPTH, D_MODEL, D_MODEL), f32) * D_MODEL ** -0.5,
        'final_norm_g': 1.0 + 0.02 * jax.random.normal(ks[13], (D_MODEL,), f32),
    }

def reference(x_prompt, x_sample, state_pool, state_conv, norm_g, w_in, b_gate, w_pool_mix,
              pool_scale, w_conv, w_proj_pool, w_proj_conv, w_out, final_norm_g):
    bp = x_prompt.shape[0]
    zero_pool = jnp.zeros((DEPTH, bp, POOL_BUF, E_POOL), x_prompt.dtype)
    zero_conv = jnp.zeros((DEPTH, bp, CONV_BUF, E_CONV), x_prompt.dtype)
    y_prompt, new_pool_prompt, new_conv_prompt = trunk(
        x_prompt, zero_pool, zero_conv, 0, norm_g, w_in, b_gate, w_pool_mix, pool_scale,
        w_conv, w_proj_pool, w_proj_conv, w_out, final_norm_g)
    y_sample, new_pool_sample, new_conv_sample = trunk(
        x_sample, state_pool, state_conv, PAST_LEN, norm_g, w_in, b_gate, w_pool_mix, pool_scale,
        w_conv, w_proj_pool, w_proj_conv, w_out, final_norm_g)
    return (y_prompt, y_sample, new_pool_prompt, new_conv_prompt, new_pool_sample, new_conv_sample)


_drawn_inputs = setup_inputs


def setup_inputs(seed=0):
    import zlib

    import numpy as np

    out = dict(_drawn_inputs(seed))
    spreads = {}
    factors = {}
    for name, (base, spread) in spreads.items():
        noise = np.random.default_rng([zlib.crc32(name.encode()), seed]).standard_normal(out[name].shape)
        drawn = base * np.exp(spread * noise) if base else spread * noise
        out[name] = __import__('jax').numpy.asarray(drawn.astype(out[name].dtype))
    for name, factor in factors.items():
        out[name] = (out[name] * factor).astype(out[name].dtype)
    return out
```

```python
from contextlib import ExitStack

import concourse.bass as bass
from concourse import mybir

F32 = mybir.dt.float32
F32R = mybir.dt.float32r
ALU = mybir.AluOpType
ACT = mybir.ActivationFunctionType

P = 128
HALVES = 2
RING = 4
EPS = 1e-6
WINDOWS = (2, 4, 8, 16)


def bass_hybrid_stream_step(nc, x_prompt, x_sample, state_pool, state_conv, norm_g, w_in, b_gate,
                            w_pool_mix, pool_scale, w_conv, w_proj_pool, w_proj_conv, w_out,
                            final_norm_g, y_prompt, y_sample, new_pool_prompt, new_conv_prompt,
                            new_pool_sample, new_conv_sample):
    _, SEQ, D = x_prompt.shape
    DEC = x_sample.shape[1]
    E = w_proj_pool.shape[1]
    POOL_BUF = state_pool.shape[2]
    CONV_BUF = state_conv.shape[2]
    TAPS = w_conv.shape[1]
    GROUP = w_pool_mix.shape[2]

    T = (SEQ + DEC) // HALVES
    HC = T // 2
    KD = D // P
    KE = E // P
    CK = 8
    CW = CK * P
    GJ = GROUP // P
    NG = E // GROUP
    TT = -(-T // P)
    TL = T - (TT - 1) * P
    CUT = SEQ - T
    MU = 4
    assert KD == 2 * CK and KE == CK and NG == len(WINDOWS) and KD % MU == 0 and GJ == 2

    SEGS = [[(0, T)], [(0, CUT), (CUT, T - CUT)]]
    PIECES = [[(0, 0, 0, HC), (1, 0, HC, HC)],
              [(0, 0, 0, HC), (1, 0, HC, CUT - HC), (1, CUT - HC, CUT, T - CUT)]]

    def ext(half, t, halo):
        return halo + t + (halo if half == 1 and t >= CUT else 0)

    B_XA, B_ZA, B_V, B_BG, B_CG, B_ZB = (k * KE for k in range(6))
    B_GA = 6 * KE
    B_GB = B_GA + KD

    one_each = {f"drained{b}": 1 for b in range(4)}
    two_each = {f"drained{b}": 2 for b in range(4)}
    PHASES = {
        "setup": (1, {"drained0": 1, "drained1": 1, "diff_made": 2}),
        "norm": (TT, {"row_squared": 1, "norm_step": 2, "x_scaled": 1}),
        "prep": (KD // 4, {**one_each, "transposed": 4, "h_hi": 4}),
        "pool": (NG, {"chunk": 8, **one_each, "drained0": 2, "drained1": 2, "mix_landed": 16,
                      "mix_w_hi": 1, "mix_w_lo": 1, "diff_made": 2, "diff_hi": 2, "diff_split": 2,
                      "za_sigmoid": 2, "mix_done": 2, "y_hi": 2, "y_split": 2}),
        "mergeA": (KD // MU, {"chunk": 3 * MU, **two_each}),
        "conv": (KE, {"chunk": 8, **one_each, "conv_step": TAPS, "zb_sigmoid": 1, "y_raw": 1,
                      "y_hi": 1, "y_split": 1}),
        "mergeB": (KD // MU, {"chunk": 3 * MU, **two_each, "merged": MU}),
        "state": (1, {"drained0": 1, "transposed": 1}),
        "split": (KD, {"merged_hi": 1, "merged_split": 1}),
        "out": (KD // 2, {"chunk": 4, **one_each, "transposed": 2}),
        "final": (TT, {"row_squared": 1, "norm_step": 2, "y_normed": 1}),
    }
    base, count = {}, {}
    for half, phase in [(0, "setup")] + [(h, p) for h in range(HALVES) for p in PHASES if p != "setup"]:
        if phase == "state" and half == 0:
            continue
        n, ticks = PHASES[phase]
        for s, k in ticks.items():
            base[s, half, phase] = count.get(s, 0)
            count[s] = count.get(s, 0) + n * k
    CHUNKS = count["chunk"]

    def at(s, half, phase, i, k):
        return base[s, half, phase] + PHASES[phase][1][s] * i + k

    with ExitStack() as ctx:
        def sem(name):
            return ctx.enter_context(nc.semaphore(name))

        def tile(name, shape, dt=F32):
            return ctx.enter_context(nc.sbuf_tensor(name, [P, *shape], dt))

        def overlay(*groups):
            out = []
            for group in groups[:-1]:
                with ExitStack() as s:
                    out.append([s.enter_context(nc.sbuf_tensor(n, [P, *shape], dt))
                                for n, shape, dt in group])
            out.append([tile(*t) for t in groups[-1]])
            return out

        (res, fin_g), (h,) = overlay(
            [("res", [TT, D], F32), ("fin_g", [D], F32)],
            [("h", [KD, 2, T], F32R)])
        ((xn,), (y, xe, ws, dr, ds, yrp, mix_raw, mix_hi, mix_lo), (_, m), (ms,)) = overlay(
            [("xn", [TT, D], F32)],
            [("y", [KE, 2, T], F32R), ("xe", [2, T + 2 * POOL_BUF], F32), ("ws", [2, T + 2 * POOL_BUF], F32),
             ("dr", [2, T], F32), ("ds", [2, 2, T], F32R), ("yrp", [2, T], F32),
             ("mix_raw", [GJ * GROUP], F32), ("mix_hi", [GJ * GROUP], F32R), ("mix_lo", [GJ * GROUP], F32R)],
            [("y_place", [KE, 2, T], F32R), ("m", [KD, T], F32)],
            [("ms", [KD, 2, T], F32R)])
        ((vec_rows, state_rows), (junk,), (za_sig, za_silu), (gate, part), (ot, so),
         (v, u, cv, q, zb_sig, zb_silu, yrc)) = overlay(
            [("vec_rows", [P], F32), ("state_rows", [E], F32)],
            [("junk", [D], F32)],
            [("za_sig", [2, T], F32), ("za_silu", [2, T], F32)],
            [("gate", [2, T], F32), ("part", [2, T], F32)],
            [("ot", [2, T], F32), ("so", [E], F32)],
            [("v", [T], F32), ("u", [T + 2 * CONV_BUF], F32), ("cv", [2, T + CONV_BUF], F32), ("q", [T], F32),
             ("zb_sig", [T], F32), ("zb_silu", [T], F32), ("yrc", [T], F32)])

        raw = tile("raw", [RING, CW])
        hi = tile("hi", [RING, CW], F32R)
        lo = tile("lo", [RING, CW], F32R)
        ident = tile("ident", [P])
        NVEC = KD + 2 * KD + KE + TAPS * KE
        vec = tile("vec", [NVEC])
        HALO = POOL_BUF + CONV_BUF
        state = tile("state", [KE, HALO])
        carry = tile("carry", [KE, HALO])
        zero = tile("zero", [HALO])
        tails = tile("tails", [KE, 2 * HALO])
        ratio = tile("ratio", [NG, POOL_BUF])
        ssq = tile("ssq", [TT])
        var = tile("var", [TT])
        rstd = tile("rstd", [TT])
        power = tile("power", [1])

        ps = [ctx.enter_context(nc.psum_tensor(f"ps{b}", [P, 2, 512], F32)) for b in range(4)]
        flat = [b[:, :, :].rearrange("p b n -> p (b n)") for b in ps]
        cols = [b[:, :, 0:HC] for b in ps]

        def two(a):
            return a.rearrange("p (b n) -> p b n", b=2)

        def f32(a):
            return a.bitcast(F32)

        V_G, V_B, V_S, V_W = 0, KD, 3 * KD, 3 * KD + KE

        def per_channel(c):
            return vec[:, bass.ds(c, 1)]

        raw_landed = [sem(f"raw_landed{s}") for s in range(RING)]
        chunk_hi = sem("chunk_hi")
        chunk_lo = sem("chunk_lo")
        chunk_done = sem("chunk_done")
        drained = [sem(f"drained{b}") for b in range(4)]
        const_set = sem("const_set")
        ident_made = sem("ident_made")
        rows_landed = sem("rows_landed")
        setup_transposed = sem("setup_transposed")
        x_landed = [sem(f"x_landed{t}") for t in range(TT)]
        row_squared = sem("row_squared")
        norm_step = sem("norm_step")
        x_scaled = sem("x_scaled")
        transposed = sem("transposed")
        h_hi = sem("h_hi")
        mix_landed = sem("mix_landed")
        mix_w_hi = sem("mix_w_hi")
        mix_w_lo = sem("mix_w_lo")
        window_step = sem("window_step")
        diff_made = sem("diff_made")
        diff_hi = sem("diff_hi")
        diff_split = sem("diff_split")
        za_sigmoid = sem("za_sigmoid")
        mix_done = sem("mix_done")
        conv_step = sem("conv_step")
        zb_sigmoid = sem("zb_sigmoid")
        y_raw = sem("y_raw")
        y_hi = sem("y_hi")
        y_split = sem("y_split")
        merged = sem("merged")
        merged_hi = sem("merged_hi")
        merged_split = sem("merged_split")
        res_landed = sem("res_landed")
        y_normed = sem("y_normed")
        y_stored = sem("y_stored")
        states_stored = sem("states_stored")

        win_v = w_in[0].rearrange("(kh kt p) (b c) -> kh b p kt c", kh=2, p=P, c=P)
        wout_v = w_out[0].rearrange("(kh kt p) (b c) -> kh b p kt c", kh=2, p=P, c=P)
        wpp_v = w_proj_pool[0].rearrange("(kt p) (b c) -> b p kt c", p=P, c=P)
        wpc_v = w_proj_conv[0].rearrange("(kt p) (b c) -> b p kt c", p=P, c=P)
        mix_v = w_pool_mix[0].rearrange("g (kt p) d -> g p kt d", p=P)

        def token_runs(half, prompt, sample):
            out = []
            for first, n in SEGS[half]:
                t = first
                while t < first + n:
                    k = min(P - t % P, first + n - t)
                    if half == 1 and t >= CUT:
                        rows = sample[0, t - CUT:t - CUT + k, :]
                    else:
                        rows = prompt[0, half * T + t:half * T + t + k, :]
                    out.append((t // P, t % P, rows))
                    t += k
            return out

        X_RUNS = [token_runs(hf, x_prompt, x_sample) for hf in range(HALVES)]
        Y_RUNS = [token_runs(hf, y_prompt, y_sample) for hf in range(HALVES)]
        x_arrived = [[16 * sum(t == tt for hf in range(half + 1) for t, _, _ in X_RUNS[hf])
                      for tt in range(TT)] for half in range(HALVES)]
        res_arrived = [16 * sum(len(r) + 1 for r in X_RUNS[:half + 1]) for half in range(HALVES)]
        stored = [16 * sum(len(r) for r in Y_RUNS[:half + 1]) for half in range(HALVES)]

        def rows_of(tt):
            return P if tt < TT - 1 else TL

        def spans(eng, half, phase, peel_first=False, peel_last=False):
            n = PHASES[phase][0]
            a, b = int(peel_first), n - int(peel_last)
            if peel_first:
                yield 0
            with eng.Fori(a, b) as i:
                yield i
            if peel_last:
                yield n - 1

        def settled(eng, half, phase):
            for b in range(4):
                eng.wait_ge(drained[b], base[f"drained{b}", half, phase])

        block = ctx.enter_context(nc.Block())

        @block.sync
        def _(sp):
            def load(n, k, src, wait=True):
                if wait:
                    sp.wait_ge(chunk_lo, n - RING + 1)
                sp.dma_start(raw[:, k % RING, :].rearrange("p (kt c) -> p kt c", c=P), src) \
                    .then_inc(raw_landed[k % RING], 16)

            for r, src in ((V_G, norm_g[0].rearrange("(r c) -> r c", c=P)),
                           (V_B, b_gate[0].rearrange("(r c) -> r c", c=P)),
                           (V_S, pool_scale[0].rearrange("(r c) -> r c", c=P)),
                           (V_W, w_conv[0].rearrange("w (r c) -> (w r) c", c=P))):
                sp.dma_start(vec_rows[r:r + src.shape[0], :], src).then_inc(rows_landed, 16)
            sp.dma_start(state_rows[0:POOL_BUF, :], state_pool[0, 0]).then_inc(rows_landed, 16)
            sp.dma_start(state_rows[POOL_BUF:HALO, :], state_conv[0, 0]).then_inc(rows_landed, 16)

            for half in range(HALVES):
                for i in spans(sp, half, "pool", peel_first=half == 0):
                    c0 = at("chunk", half, "pool", i, 0)
                    for k in range(8):
                        blk = (B_XA, B_ZA)[k // 4] + (k // 2) % 2
                        load(c0 + k, k, win_v[k % 2, 2 * i + blk], wait=not (isinstance(i, int) and k < RING))
                        if k == 3:
                            if half == 1:
                                sp.wait_ge(chunk_done, base["chunk", half, "pool"])
                            if not isinstance(i, int):
                                sp.wait_ge(mix_w_lo, at("mix_w_lo", half, "pool", i, 0))
                            sp.dma_start(mix_raw[:, :].rearrange("p (kt d) -> p kt d", d=GROUP), mix_v[i]) \
                                .then_inc(mix_landed, 16)
                for i in spans(sp, half, "mergeA"):
                    c0 = at("chunk", half, "mergeA", i, 0)
                    for k in range(3 * MU):
                        mb = MU * i + k // 3
                        load(c0 + k, k, wpp_v[mb] if k % 3 == 0 else win_v[k % 3 - 1, B_GA + mb])
                for i in spans(sp, half, "conv"):
                    c0 = at("chunk", half, "conv", i, 0)
                    for k in range(8):
                        load(c0 + k, k, win_v[k % 2, (B_V, B_CG, B_BG, B_ZB)[k // 2] + i])
                for i in spans(sp, half, "mergeB"):
                    c0 = at("chunk", half, "mergeB", i, 0)
                    for k in range(3 * MU):
                        mb = MU * i + k // 3
                        load(c0 + k, k, wpc_v[mb] if k % 3 == 0 else win_v[k % 3 - 1, B_GB + mb])
                for i in spans(sp, half, "out"):
                    c0 = at("chunk", half, "out", i, 0)
                    for k in range(4):
                        load(c0 + k, k, wout_v[k % 2, 2 * i + k // 2])

        @block.gpsimd
        def _(pool):
            nc.gpsimd.memset(ident[:, :], 0.0).then_inc(ident_made, 1)
            pool.wait_ge(ident_made, 1)
            nc.gpsimd.affine_select(out=ident[:, :], in_=ident[:, :], compare_op=ALU.not_equal, fill=1.0,
                                    base=0, pattern=[[-1, P]], channel_multiplier=1).then_inc(ident_made, 1)
            nc.gpsimd.memset(zero[:, :], 0.0).then_inc(const_set, 1)
            nc.gpsimd.memset(ratio[:, :, :], 1.0).then_inc(const_set, 1)
            pool.wait_ge(const_set, 2)
            for g, w in enumerate(WINDOWS):
                for t in range(w - 1):
                    last = nc.gpsimd.memset(ratio[:, g, t:t + 1], w / (t + 1))
            last.then_inc(const_set, 1)
            nc.gpsimd.memset(power[:, :], -0.5).then_inc(const_set, 1)
            pool.wait_ge(const_set, 4)
            for half in range(HALVES):
                for phase in ("norm", "final"):
                    for tt in range(TT):
                        r = rows_of(tt)
                        pool.wait_ge(norm_step, at("norm_step", half, phase, tt, 1))
                        nc.gpsimd.tensor_tensor(rstd[0:r, tt:tt + 1], var[0:r, tt:tt + 1], power[0:r, :], ALU.pow) \
                            .then_inc(norm_step, 1)

        @block.tensor
        def _(pe):
            def buffer(b, half, phase, i, use):
                pe.wait_ge(drained[b], at(f"drained{b}", half, phase, i, use))

            def product(b, n, k, rhs, start, stop, each=None):
                pe.wait_ge(chunk_lo, n + 1)
                s = k % RING
                for kt in range(CK):
                    if each is not None:
                        each(kt)
                    for w, part in ((hi, 0), (hi, 1), (lo, 0)):
                        for c in range(2):
                            first = start and kt == 0 and w is hi and part == 0
                            last = stop and kt == CK - 1 and w is lo
                            mm = nc.tensor.matmul(ps[b][:, c, 0:HC], w[:, s, kt * P:(kt + 1) * P],
                                                  rhs(kt, part)[:, c * HC:(c + 1) * HC], start=first, stop=last)
                mm.then_inc(chunk_done, 1)

            def full(b, half, phase, i, k, src, each=None):
                n = at("chunk", half, phase, i, k)
                for kh in range(2):
                    product(b, n + kh, k + kh, lambda kt, part: src[:, CK * kh + kt, part, :], kh == 0, kh == 1,
                            None if each is None else lambda kt: each(CK * kh + kt))

            pe.wait_ge(ident_made, 2)
            pe.wait_ge(rows_landed, 96)
            nc.tensor.transpose(flat[0][:, 0:NVEC], vec_rows[0:NVEC, :], ident[0:NVEC, 0:NVEC]) \
                .then_inc(setup_transposed, 1)
            for j in range(KE):
                last = nc.tensor.transpose(flat[1][:, 32 * j:32 * j + HALO], state_rows[0:HALO, j * P:(j + 1) * P],
                                           ident[0:HALO, 0:HALO])
            last.then_inc(setup_transposed, 1)

            for half in range(HALVES):
                pe.wait_ge(x_scaled, at("x_scaled", half, "norm", TT, 0))
                for kt in range(KD):
                    i, b = divmod(kt, 4)
                    buffer(b, half, "prep", i, 0)
                    for tt in range(TT):
                        r = rows_of(tt)
                        last = nc.tensor.transpose(flat[b][:, tt * P:tt * P + r], xn[0:r, tt, kt * P:(kt + 1) * P],
                                                   ident[0:r, 0:r])
                    last.then_inc(transposed, 1)
                for b in range(4):
                    buffer(b, half, "pool", 0, 0)

                for i in spans(pe, half, "pool"):
                    for k, b in ((0, 0), (2, 1), (4, 2), (6, 3)):
                        buffer(b, half, "pool", i, 0)
                        full(b, half, "pool", i, k, h)
                    pe.wait_ge(mix_w_lo, at("mix_w_lo", half, "pool", i, 1))
                    pe.wait_ge(diff_split, at("diff_split", half, "pool", i, 2))
                    for j in range(GJ):
                        buffer(j, half, "pool", i, 1)
                        for kt in range(GJ):
                            for w, part in ((mix_hi, 0), (mix_hi, 1), (mix_lo, 0)):
                                for c in range(2):
                                    mm = nc.tensor.matmul(
                                        ps[j][:, c, 0:HC], w[:, kt * GROUP + j * P:kt * GROUP + (j + 1) * P],
                                        ds[:, kt, part, c * HC:(c + 1) * HC],
                                        start=kt == 0 and w is mix_hi and part == 0,
                                        stop=kt == GJ - 1 and w is mix_lo)
                        mm.then_inc(mix_done, 1)

                def merge(phase):
                    last_y = {"mergeA": ("pool", NG), "mergeB": ("conv", KE)}[phase]
                    pe.wait_ge(y_split, at("y_split", half, *last_y, 0))
                    for i in spans(pe, half, phase):
                        for ii in range(MU):
                            b = 2 * (ii % 2)
                            buffer(b, half, phase, i, ii // 2)
                            product(b, at("chunk", half, phase, i, 3 * ii), 3 * ii,
                                    lambda kt, part: y[:, kt, part, :], True, True)
                            buffer(b + 1, half, phase, i, ii // 2)
                            full(b + 1, half, phase, i, 3 * ii + 1, h)

                merge("mergeA")
                for i in spans(pe, half, "conv"):
                    for b in range(4):
                        buffer(b, half, "conv", i, 0)
                        full(b, half, "conv", i, 2 * b, h)
                merge("mergeB")

                if half == 1:
                    pe.wait_ge(zb_sigmoid, at("zb_sigmoid", half, "conv", KE, 0))
                    buffer(0, half, "state", 0, 0)
                    for j in range(KE):
                        last = nc.tensor.transpose(flat[0][0:2 * HALO, j * P:(j + 1) * P], tails[:, j, :],
                                                   ident[:, :])
                    last.then_inc(transposed, 1)

                def back(i, e):
                    pe.wait_ge(drained[e], at(f"drained{e}", half, "out", i, 1))
                    buffer(2 + e, half, "out", i, 0)
                    for tt in range(TT):
                        r = rows_of(tt)
                        last = nc.tensor.transpose(flat[2 + e][0:r, tt * P:(tt + 1) * P],
                                                   ot[:, e, tt * P:tt * P + r], ident[:, :])
                    last.then_inc(transposed, 1)

                for i in spans(pe, half, "out", peel_first=True):
                    first = isinstance(i, int)
                    each = None
                    if first:
                        each = lambda kt: pe.wait_ge(merged_split, at("merged_split", half, "split", kt, 1))
                    buffer(0, half, "out", i, 0)
                    full(0, half, "out", i, 0, ms, each)
                    if not first:
                        back(i - 1, 1)
                    buffer(1, half, "out", i, 0)
                    full(1, half, "out", i, 2, ms)
                    back(i, 0)
                back(PHASES["out"][0] - 1, 1)

        @block.scalar
        def _(act):
            def ahead(half, phase, i, k):
                n = at("chunk", half, phase, i, k)
                act.wait_ge(chunk_done, n + 1)
                s = k % RING
                act.wait_ge(raw_landed[s], (16 // RING) * (n - s) + 32)
                nc.scalar.activation(hi[:, s, :], raw[:, s, :], ACT.Copy).then_inc(chunk_hi, 1)

            def done(half, phase, i, k):
                act.wait_ge(chunk_done, at("chunk", half, phase, i, k) + 1)

            def load_rows(half, dst, sems):
                for (tt, p0, rows), s in zip(X_RUNS[half], sems):
                    act.dma_start(dst[p0:p0 + rows.shape[0], tt, :], rows).then_inc(s, 16)

            load_rows(0, xn, [x_landed[tt] for tt, _, _ in X_RUNS[0]])
            for s in range(RING):
                act.wait_ge(raw_landed[s], 16)
                nc.scalar.activation(hi[:, s, :], raw[:, s, :], ACT.Copy).then_inc(chunk_hi, 1)
            act.wait_ge(drained[0], 1)
            act.wait_ge(drained[1], 1)
            act.wait_ge(const_set, 3)

            for half in range(HALVES):
                for tt in range(TT):
                    r = rows_of(tt)
                    act.wait_ge(x_landed[tt], x_arrived[half][tt])
                    if tt > 0:
                        act.wait_ge(row_squared, at("row_squared", half, "norm", tt, 0))
                    nc.scalar.activation(junk[0:r, :], xn[0:r, tt, :], ACT.Square,
                                         accum_out=ssq[0:r, tt:tt + 1]).then_inc(row_squared, 1)
                if half == 1:
                    act.wait_ge(y_stored, stored[half - 1])
                for i in spans(act, half, "prep"):
                    for b in range(4):
                        kt = 4 * i + b
                        act.wait_ge(transposed, at("transposed", half, "prep", i, b + 1))
                        nc.scalar.activation(h[:, kt, 0, :], flat[b][:, 0:T], ACT.Copy,
                                             scale=per_channel(V_G + kt)).then_inc(h_hi, 1)

                settled(act, half, "pool")
                for i in spans(act, half, "pool"):
                    for k in range(8):
                        ahead(half, "pool", i, k)
                        if k == 4:
                            act.wait_ge(mix_landed, at("mix_landed", half, "pool", i, 16))
                            nc.scalar.activation(mix_hi[:, :], mix_raw[:, :], ACT.Copy).then_inc(mix_w_hi, 1)
                        if k in (1, 3):
                            j = k // 2
                            act.wait_ge(diff_made, at("diff_made", half, "pool", i, j + 1 - 2))
                            jb = 2 * i + j
                            left = zero[:, 0:POOL_BUF] if half == 0 else carry[:, jb, 0:POOL_BUF]
                            nc.scalar.copy(xe[:, j, 0:POOL_BUF], left)
                            if half == 1:
                                c = ext(1, CUT, POOL_BUF) - POOL_BUF
                                nc.scalar.copy(xe[:, j, c:c + POOL_BUF], state[:, jb, 0:POOL_BUF])
                            for s, (first, n) in enumerate(SEGS[half]):
                                c = first + n - POOL_BUF - HC
                                dst = carry[:, jb, 0:POOL_BUF] if half == 0 else \
                                    tails[:, jb, s * POOL_BUF:(s + 1) * POOL_BUF]
                                nc.scalar.copy(dst, ps[j][:, 1, c:c + POOL_BUF])
                            for bank, c, first, n in PIECES[half]:
                                e0 = ext(half, first, POOL_BUF)
                                last = nc.scalar.copy(xe[:, j, e0:e0 + n], ps[j][:, bank, c:c + n])
                            last.then_inc(drained[j], 1)
                        if k in (2, 4):
                            j = k // 2 - 1
                            act.wait_ge(diff_made, at("diff_made", half, "pool", i, j + 1))
                            nc.scalar.copy(ds[:, j, 0, :], dr[:, j, :]).then_inc(diff_hi, 1)
                        if k in (5, 7):
                            j = (k - 5) // 2
                            nc.scalar.activation(za_sig[:, j, :].rearrange("p (b n) -> p b n", b=2), cols[2 + j],
                                                 ACT.Sigmoid).then_inc(za_sigmoid, 1)
                    for j in range(GJ):
                        act.wait_ge(drained[j], at(f"drained{j}", half, "pool", i, 2))
                        nc.scalar.copy(y[:, 2 * i + j, 0, :], yrp[:, j, :]).then_inc(y_hi, 1)

                def merge(phase, bias0):
                    settled(act, half, phase)
                    for i in spans(act, half, phase):
                        for k in range(3 * MU):
                            ahead(half, phase, i, k)
                            if k % 3 == 2:
                                ii = k // 3
                                g = ii % 2
                                nc.scalar.activation(two(gate[:, g, :]), cols[2 * g + 1], ACT.Sigmoid,
                                                     bias=per_channel(bias0 + MU * i + ii)) \
                                    .then_inc(drained[2 * g + 1], 1)

                merge("mergeA", V_B)

                settled(act, half, "conv")
                for i in spans(act, half, "conv"):
                    for k in range(8):
                        ahead(half, "conv", i, k)
                        if k == 1:
                            left = zero[:, 0:CONV_BUF] if half == 0 else carry[:, i, POOL_BUF:HALO]
                            nc.scalar.copy(u[:, 0:CONV_BUF], left)
                            if half == 1:
                                c = ext(1, CUT, CONV_BUF) - CONV_BUF
                                nc.scalar.copy(u[:, c:c + CONV_BUF], state[:, i, POOL_BUF:HALO])
                            nc.scalar.copy(two(v[:, :]), cols[0]).then_inc(drained[0], 1)
                        if k == 4:
                            act.wait_ge(drained[1], at("drained1", half, "conv", i, 1))
                            for s, (first, n) in enumerate(SEGS[half]):
                                c = ext(half, first + n - 1, CONV_BUF) + 1 - CONV_BUF
                                d0 = 2 * POOL_BUF + s * CONV_BUF
                                dst = carry[:, i, POOL_BUF:HALO] if half == 0 else tails[:, i, d0:d0 + CONV_BUF]
                                nc.scalar.copy(dst, u[:, c:c + CONV_BUF])
                        if k == 7:
                            nc.scalar.activation(two(zb_sig[:, :]), cols[3], ACT.Sigmoid).then_inc(zb_sigmoid, 1)
                    act.wait_ge(y_raw, at("y_raw", half, "conv", i, 1))
                    nc.scalar.copy(y[:, i, 0, :], yrc[:, :]).then_inc(y_hi, 1)

                merge("mergeB", V_B + KD)

                act.wait_ge(chunk_done, base["chunk", half, "out"])
                load_rows(half, res, [res_landed] * len(X_RUNS[half]))
                act.dma_start(fin_g[:, :], final_norm_g.rearrange("(a d) -> a d", a=1)
                              .broadcast_to([P, D])).then_inc(res_landed, 16)
                act.wait_ge(merged, at("merged", half, "mergeB", PHASES["mergeB"][0], 0))
                for s in range(KD):
                    if 2 * s >= KD:
                        act.wait_ge(merged_split, at("merged_split", half, "split", 2 * s - KD, 1))
                    nc.scalar.copy(ms[:, s, 0, :], m[:, s, :]).then_inc(merged_hi, 1)
                if half == 1:
                    act.wait_ge(drained[0], at("drained0", half, "state", 0, 1))
                    r = 0
                    for dst in (new_pool_prompt, new_pool_sample, new_conv_prompt, new_conv_sample):
                        n = dst.shape[2]
                        act.dma_start(dst[0, 0], so[r:r + n, :]).then_inc(states_stored, 16)
                        r += n

                for i in spans(act, half, "out", peel_last=half == 1):
                    for k in range(4):
                        if half == 1 and isinstance(i, int):
                            done(half, "out", i, k)
                        else:
                            ahead(half, "out", i, k)
                        if k % 2 == 1:
                            e = k // 2
                            nc.scalar.copy(two(ot[:, e, :]), cols[e]).then_inc(drained[e], 1)

                for b in (2, 3):
                    act.wait_ge(drained[b], at(f"drained{b}", half, "out", PHASES["out"][0], 0))
                if half == 1:
                    act.wait_ge(states_stored, 64)
                if half == 0:
                    load_rows(1, xn, [x_landed[tt] for tt, _, _ in X_RUNS[1]])
                for tt in range(TT):
                    r = rows_of(tt)
                    if tt > 0:
                        act.wait_ge(row_squared, at("row_squared", half, "final", tt, 0))
                    nc.scalar.activation(junk[0:r, :], res[0:r, tt, :], ACT.Square,
                                         accum_out=ssq[0:r, tt:tt + 1]).then_inc(row_squared, 1)
                for tt, p0, rows in Y_RUNS[half]:
                    act.wait_ge(y_normed, at("y_normed", half, "final", tt, 1))
                    act.dma_start(rows, res[p0:p0 + rows.shape[0], tt, :]).then_inc(y_stored, 16)
            act.wait_ge(y_stored, stored[-1])

        @block.vector
        def _(dve):
            def split(n, s):
                dve.wait_ge(chunk_hi, n + 1)
                nc.vector.tensor_tensor(lo[:, s, :], raw[:, s, :], f32(hi[:, s, :]), ALU.subtract) \
                    .then_inc(chunk_lo, 1)

            def ahead(half, phase, i, k):
                split(at("chunk", half, phase, i, k) + RING, k % RING)

            def rsqrt(half, phase, tt, r):
                dve.wait_ge(row_squared, at("row_squared", half, phase, tt, 1))
                nc.vector.tensor_scalar(var[0:r, tt:tt + 1], ssq[0:r, tt:tt + 1], 1.0 / D, EPS, ALU.mult, ALU.add) \
                    .then_inc(norm_step, 1)
                dve.wait_ge(norm_step, at("norm_step", half, phase, tt, 1))
                dve.wait_ge(norm_step, at("norm_step", half, phase, tt, 2))

            def y_lo(half, phase, i, k, jb, src):
                dve.wait_ge(y_hi, at("y_hi", half, phase, i, k))
                nc.vector.tensor_tensor(y[:, jb, 1, :], src, f32(y[:, jb, 0, :]), ALU.subtract) \
                    .then_inc(y_split, 1)

            steps = [0]

            def window_link(ins):
                steps[0] += 1
                ins.then_inc(window_step, 1)
                dve.wait_ge(window_step, steps[0])

            dve.wait_ge(setup_transposed, 1)
            nc.vector.tensor_copy(vec[:, :], flat[0][:, 0:NVEC]).then_inc(drained[0], 1)
            dve.wait_ge(setup_transposed, 2)
            nc.vector.tensor_copy(state[:, :, :], flat[1][:, 0:32 * KE].rearrange("p (j n) -> p j n", n=32)
                                  [:, :, 0:HALO]).then_inc(drained[1], 1)
            nc.vector.memset(var[:, :], 0.0).then_inc(diff_made, 2)
            for s in range(RING):
                split(s, s)
            dve.wait_ge(drained[0], 1)
            dve.wait_ge(drained[1], 1)
            dve.wait_ge(const_set, 3)
            dve.wait_ge(diff_made, 2)

            for half in range(HALVES):
                for tt in range(TT):
                    r = rows_of(tt)
                    rsqrt(half, "norm", tt, r)
                    nc.vector.tensor_scalar(xn[0:r, tt, :], xn[0:r, tt, :], rstd[0:r, tt:tt + 1], None, ALU.mult) \
                        .then_inc(x_scaled, 1)
                for i in spans(dve, half, "prep"):
                    for b in range(4):
                        kt = 4 * i + b
                        dve.wait_ge(h_hi, at("h_hi", half, "prep", i, b + 1))
                        nc.vector.scalar_tensor_tensor(h[:, kt, 1, :], flat[b][:, 0:T], per_channel(V_G + kt),
                                                       f32(h[:, kt, 0, :]), ALU.mult, ALU.subtract) \
                            .then_inc(drained[b], 1)

                for g, w in enumerate(WINDOWS):
                    for k in range(8):
                        ahead(half, "pool", g, k)
                        if k == 4:
                            dve.wait_ge(mix_w_hi, at("mix_w_hi", half, "pool", g, 1))
                            nc.vector.tensor_tensor(mix_lo[:, :], mix_raw[:, :], f32(mix_hi[:, :]), ALU.subtract) \
                                .then_inc(mix_w_lo, 1)
                        if k in (1, 3):
                            j = k // 2
                            width = ext(half, T - 1, POOL_BUF) + 1
                            dve.wait_ge(drained[j], at(f"drained{j}", half, "pool", g, 1))
                            src, reach, n = xe[:, j, :], 0, 1
                            while n < w:
                                dst = ws[:, n.bit_length() % 2, :]
                                lo_c = reach + n
                                window_link(nc.vector.tensor_tensor(
                                    dst[:, lo_c:width], src[:, lo_c:width], src[:, lo_c - n:width - n], ALU.add))
                                src, reach, n = dst, lo_c, 2 * n
                            if half == 0:
                                s0 = src[:, POOL_BUF:2 * POOL_BUF]
                                window_link(nc.vector.tensor_tensor(s0, s0, ratio[:, g, :], ALU.mult))
                            for first, n in SEGS[half]:
                                e0 = ext(half, first, POOL_BUF)
                                last = nc.vector.scalar_tensor_tensor(
                                    dr[:, j, first:first + n], src[:, e0:e0 + n], 1.0 / w, xe[:, j, e0:e0 + n],
                                    ALU.mult, ALU.subtract)
                            last.then_inc(diff_made, 1)
                        if k in (2, 4):
                            j = k // 2 - 1
                            dve.wait_ge(diff_hi, at("diff_hi", half, "pool", g, j + 1))
                            nc.vector.tensor_tensor(ds[:, j, 1, :], dr[:, j, :], f32(ds[:, j, 0, :]), ALU.subtract) \
                                .then_inc(diff_split, 1)
                        if k in (5, 7):
                            j = (k - 5) // 2
                            dve.wait_ge(za_sigmoid, at("za_sigmoid", half, "pool", g, j + 1))
                            nc.vector.tensor_tensor(two(za_silu[:, j, :]), cols[2 + j], two(za_sig[:, j, :]),
                                                    ALU.mult).then_inc(drained[2 + j], 1)
                    for j in range(GJ):
                        dve.wait_ge(mix_done, at("mix_done", half, "pool", g, j + 1))
                        dve.wait_ge(drained[2 + j], at(f"drained{2 + j}", half, "pool", g, 1))
                        nc.vector.scalar_tensor_tensor(two(yrp[:, j, :]), cols[j], per_channel(V_S + 2 * g + j),
                                                       two(za_silu[:, j, :]), ALU.mult, ALU.mult) \
                            .then_inc(drained[j], 1)
                    for j in range(GJ):
                        y_lo(half, "pool", g, j + 1, 2 * g + j, yrp[:, j, :])

                for i in spans(dve, half, "mergeA"):
                    for k in range(3 * MU):
                        ahead(half, "mergeA", i, k)
                        if k % 3 == 2:
                            ii = k // 3
                            b = 2 * (ii % 2)
                            dve.wait_ge(drained[b + 1], at(f"drained{b + 1}", half, "mergeA", i, ii // 2 + 1))
                            nc.vector.tensor_tensor(two(m[:, MU * i + ii, :]), cols[b], two(gate[:, ii % 2, :]),
                                                    ALU.mult).then_inc(drained[b], 1)

                for i in spans(dve, half, "conv"):
                    width = ext(half, T - 1, CONV_BUF) + 1 - CONV_BUF
                    for k in range(8):
                        ahead(half, "conv", i, k)
                        if k == 3:
                            dve.wait_ge(drained[0], at("drained0", half, "conv", i, 1))
                            for bank, c, first, n in PIECES[half]:
                                e0 = ext(half, first, CONV_BUF)
                                last = nc.vector.tensor_tensor(u[:, e0:e0 + n], ps[1][:, bank, c:c + n],
                                                               v[:, first:first + n], ALU.mult)
                            last.then_inc(drained[1], 1)
                            dve.wait_ge(drained[1], at("drained1", half, "conv", i, 1))
                            tap = [per_channel(V_W + KE * w + i) for w in range(TAPS)]
                            nc.vector.tensor_scalar(cv[:, 0, 0:width], u[:, 0:width], tap[0], None, ALU.mult) \
                                .then_inc(conv_step, 1)
                            for w in range(1, TAPS):
                                dve.wait_ge(conv_step, at("conv_step", half, "conv", i, w))
                                nc.vector.scalar_tensor_tensor(cv[:, w % 2, 0:width], u[:, w:w + width], tap[w],
                                                               cv[:, (w - 1) % 2, 0:width], ALU.mult, ALU.add) \
                                    .then_inc(conv_step, 1)
                        if k == 5:
                            dve.wait_ge(conv_step, at("conv_step", half, "conv", i, TAPS))
                            for bank, c, first, n in PIECES[half]:
                                e0 = ext(half, first, CONV_BUF) - CONV_BUF
                                last = nc.vector.tensor_tensor(q[:, first:first + n], ps[2][:, bank, c:c + n],
                                                               cv[:, (TAPS - 1) % 2, e0:e0 + n], ALU.mult)
                            last.then_inc(drained[2], 1)
                        if k == 7:
                            dve.wait_ge(zb_sigmoid, at("zb_sigmoid", half, "conv", i, 1))
                            nc.vector.tensor_tensor(two(zb_silu[:, :]), cols[3], two(zb_sig[:, :]), ALU.mult) \
                                .then_inc(drained[3], 1)
                            for b in (2, 3):
                                dve.wait_ge(drained[b], at(f"drained{b}", half, "conv", i, 1))
                            nc.vector.tensor_tensor(yrc[:, :], q[:, :], zb_silu[:, :], ALU.mult).then_inc(y_raw, 1)
                    y_lo(half, "conv", i, 1, i, yrc[:, :])

                for i in spans(dve, half, "mergeB"):
                    for k in range(3 * MU):
                        ahead(half, "mergeB", i, k)
                        if k % 3 == 2:
                            ii = k // 3
                            b = 2 * (ii % 2)
                            dve.wait_ge(drained[b + 1], at(f"drained{b + 1}", half, "mergeB", i, ii // 2 + 1))
                            nc.vector.tensor_tensor(two(part[:, ii % 2, :]), cols[b], two(gate[:, ii % 2, :]),
                                                    ALU.mult).then_inc(drained[b], 1)
                            dve.wait_ge(drained[b], at(f"drained{b}", half, "mergeB", i, ii // 2 + 1))
                            mb = m[:, MU * i + ii, :]
                            nc.vector.tensor_tensor(mb, mb, part[:, ii % 2, :], ALU.add).then_inc(merged, 1)

                for s in range(KD):
                    dve.wait_ge(merged_hi, at("merged_hi", half, "split", s, 1))
                    if 2 * s >= KD:
                        dve.wait_ge(merged_split, at("merged_split", half, "split", min(2 * s - KD + 1, s - 1), 1))
                    nc.vector.tensor_tensor(ms[:, s, 1, :], m[:, s, :], f32(ms[:, s, 0, :]), ALU.subtract) \
                        .then_inc(merged_split, 1)
                if half == 1:
                    dve.wait_ge(transposed, at("transposed", half, "state", 0, 1))
                    nc.vector.tensor_copy(so[0:2 * HALO, :], flat[0][0:2 * HALO, 0:E]).then_inc(drained[0], 1)

                def add(i, e):
                    dve.wait_ge(transposed, at("transposed", half, "out", i, e + 1))
                    c = (2 * i + e) * P
                    a = res[:, 0:TT - 1, bass.ds(c, P)]
                    nc.vector.tensor_tensor(a, a, flat[2 + e][:, 0:(TT - 1) * P].rearrange("p (t n) -> p t n", n=P),
                                            ALU.add)
                    a = res[0:TL, TT - 1, bass.ds(c, P)]
                    nc.vector.tensor_tensor(a, a, flat[2 + e][0:TL, (TT - 1) * P:TT * P], ALU.add) \
                        .then_inc(drained[2 + e], 1)

                dve.wait_ge(res_landed, res_arrived[half])
                peel_last = half == 1
                for i in spans(dve, half, "out", peel_first=True, peel_last=peel_last):
                    first = isinstance(i, int) and i == 0
                    more = not (peel_last and isinstance(i, int) and i > 0)
                    for k in range(4):
                        if more:
                            ahead(half, "out", i, k)
                        if k == 1 and not first:
                            add(i - 1, 1)
                        if k == 3:
                            add(i, 0)
                add(PHASES["out"][0] - 1, 1)
                for b in (2, 3):
                    dve.wait_ge(drained[b], at(f"drained{b}", half, "out", PHASES["out"][0], 0))

                for tt in range(TT):
                    r = rows_of(tt)
                    rsqrt(half, "final", tt, r)
                    nc.vector.scalar_tensor_tensor(res[0:r, tt, :], res[0:r, tt, :], rstd[0:r, tt:tt + 1],
                                                   fin_g[0:r, :], ALU.mult, ALU.mult).then_inc(y_normed, 1)


_INS = ['x_prompt', 'x_sample', 'state_pool', 'state_conv', 'norm_g', 'w_in', 'b_gate', 'w_pool_mix',
        'pool_scale', 'w_conv', 'w_proj_pool', 'w_proj_conv', 'w_out', 'final_norm_g']


def kernel(**inputs):
    import numpy as _np
    import concourse.bacc as _bacc
    from concourse import mybir as _mybir
    from concourse.bass_utils import run_bass_kernel_spmd as _run

    nc = _bacc.Bacc("TRN2", target_bir_lowering=False, num_devices=1)
    arrays, args = {}, []
    for name in _INS:
        a = _np.ascontiguousarray(inputs[name])
        arrays[f"in_{name}_dram"] = a
        args.append(nc.dram_tensor(f"in_{name}_dram", a.shape, _mybir.dt.from_np(a.dtype), kind="ExternalInput").ap())
    depth, _, pool_buf, e_pool = inputs['state_pool'].shape
    conv_buf, e_conv = inputs['state_conv'].shape[2:]
    b, db = inputs['x_prompt'].shape[0], inputs['x_sample'].shape[0]
    outs = [inputs['x_prompt'].shape, inputs['x_sample'].shape, (depth, b, pool_buf, e_pool),
            (depth, b, conv_buf, e_conv), (depth, db, pool_buf, e_pool), (depth, db, conv_buf, e_conv)]
    for i, shape in enumerate(outs):
        args.append(nc.dram_tensor(f"out_{i}_dram", tuple(shape), _mybir.dt.float32, kind="ExternalOutput").ap())
    bass_hybrid_stream_step(nc, *args)
    r = _run(nc, [arrays], core_ids=[0])
    return tuple(r.results[0][f"out_{i}_dram"] for i in range(len(outs)))
```

```python
from contextlib import ExitStack

import concourse.bass as bass
from concourse import mybir

F32 = mybir.dt.float32
F32R = mybir.dt.float32r
ALU = mybir.AluOpType
ACT = mybir.ActivationFunctionType

P = 128
HALVES = 2
RING = 4
EPS = 1e-6
WINDOWS = (2, 4, 8, 16)


def bass_hybrid_stream_step(nc, x_prompt, x_sample, state_pool, state_conv, norm_g, w_in, b_gate,
                            w_pool_mix, pool_scale, w_conv, w_proj_pool, w_proj_conv, w_out,
                            final_norm_g, y_prompt, y_sample, new_pool_prompt, new_conv_prompt,
                            new_pool_sample, new_conv_sample):
    _, SEQ, D = x_prompt.shape
    DEC = x_sample.shape[1]
    E = w_proj_pool.shape[1]
    POOL_BUF = state_pool.shape[2]
    CONV_BUF = state_conv.shape[2]
    TAPS = w_conv.shape[1]
    GROUP = w_pool_mix.shape[2]

    T = (SEQ + DEC) // HALVES
    HC = T // 2
    KD = D // P
    KE = E // P
    CK = 8
    CW = CK * P
    GJ = GROUP // P
    NG = E // GROUP
    TT = -(-T // P)
    TL = T - (TT - 1) * P
    CUT = SEQ - T
    MU = 4
    assert KD == 2 * CK and KE == CK and NG == len(WINDOWS) and KD % MU == 0 and GJ == 2

    SEGS = [[(0, T)], [(0, CUT), (CUT, T - CUT)]]
    PIECES = [[(0, 0, 0, HC), (1, 0, HC, HC)],
              [(0, 0, 0, HC), (1, 0, HC, CUT - HC), (1, CUT - HC, CUT, T - CUT)]]

    def ext(half, t, halo):
        return halo + t + (halo if half == 1 and t >= CUT else 0)

    B_XA, B_ZA, B_V, B_BG, B_CG, B_ZB = (k * KE for k in range(6))
    B_GA = 6 * KE
    B_GB = B_GA + KD

    ROLES = [(ii, r) for ii in range(MU) for r in ((0, 1, 2) if ii < MU - 1 else (2, 0, 1))]
    EARLY = KD // 2

    one_each = {f"drained{b}": 1 for b in range(4)}
    two_each = {f"drained{b}": 2 for b in range(4)}
    PHASES = {
        "setup": (1, {"drained0": 1, "drained1": 1, "diff_made": 2}),
        "norm": (TT, {"row_squared": 1, "norm_step": 2, "x_scaled": 1}),
        "prep": (KD, {"h_turned": 1, "h_hi": 1}),
        "pool": (NG, {"chunk": 8, **one_each, "drained0": 2, "drained1": 2, "mix_landed": 16,
                      "mix_w_hi": 1, "mix_w_lo": 1, "diff_made": 2, "diff_hi": 2, "diff_split": 2,
                      "za_sigmoid": 2, "mix_done": 2, "y_hi": 2, "y_split": 2}),
        "mergeA": (KD // MU, {"chunk": 3 * MU, **two_each}),
        "conv": (KE, {"chunk": 8, **one_each, "conv_step": TAPS, "zb_sigmoid": 1, "y_raw": 1,
                      "y_hi": 1, "y_split": 1}),
        "mergeB": (KD // MU, {"chunk": 3 * MU, **two_each, "merged": MU}),
        "state": (1, {"drained3": 1, "states_turned": 1}),
        "split": (KD, {"merged_hi": 1, "merged_split": 1}),
        "out0": (KD // 2, {"chunk": 4, "drained0": 1, "drained1": 1, "drained2": 2, "drained3": 2,
                           "turned_back": 2, "sum_step": 4, "sum_made": 2, "h_turned": 2, "h_hi": 2,
                           "xk_scaled": 2}),
        "out1": (KD // 2, {"chunk": 4, **one_each, "turned_back": 2, "sum_step": 4, "sum_made": 2}),
        "final": (1, {"norm_step": 3}),
    }
    COURSE = [[(0, p) for p in ("setup", "norm", "prep", "pool", "mergeA", "conv", "mergeB", "split",
                                "out0", "final")],
              [(1, p) for p in ("pool", "mergeA", "conv", "mergeB", "state", "split", "out1", "final")]]
    TURNS = 3
    base, count = {}, {}
    for half, phase in COURSE[0] + COURSE[1]:
        n, ticks = PHASES[phase]
        for s, k in ticks.items():
            base[s, half, phase] = count.get(s, 0)
            count[s] = count.get(s, 0) + n * k
        if phase == "prep":
            for b in range(TURNS):
                s = f"drained{1 + b}"
                base[s, half, phase] = count.get(s, 0)
                count[s] = count.get(s, 0) + len(range(b, KD, TURNS))
    CHUNKS = count["chunk"]

    def at(s, half, phase, i, k):
        return base[s, half, phase] + PHASES[phase][1][s] * i + k

    with ExitStack() as ctx:
        def sem(name):
            return ctx.enter_context(nc.semaphore(name))

        def tile(name, shape, dt=F32):
            return ctx.enter_context(nc.sbuf_tensor(name, [P, *shape], dt))

        def overlay(*groups):
            out = []
            for group in groups[:-1]:
                with ExitStack() as s:
                    out.append([s.enter_context(nc.sbuf_tensor(n, [P, *shape], dt))
                                for n, shape, dt in group])
            out.append([tile(*t) for t in groups[-1]])
            return out

        (res, fin_g), (junk,), (h,) = overlay(
            [("res", [TT, D], F32), ("fin_g", [D], F32)],
            [("junk", [D], F32)],
            [("h", [KD, 2, T], F32R)])
        ((xn,), (y, xe, ws, dr, ds, yrp, mix_raw, mix_hi, mix_lo), (_, m), (ms,)) = overlay(
            [("xn", [TT, D], F32)],
            [("y", [KE, 2, T], F32R), ("xe", [2, T + 2 * POOL_BUF], F32), ("ws", [2, T + 2 * POOL_BUF], F32),
             ("dr", [2, T], F32), ("ds", [2, 2, T], F32R), ("yrp", [2, T], F32),
             ("mix_raw", [GJ * GROUP], F32), ("mix_hi", [GJ * GROUP], F32R), ("mix_lo", [GJ * GROUP], F32R)],
            [("y_place", [KE, 2, T], F32R), ("m", [KD, T], F32)],
            [("ms", [KD, 2, T], F32R)])
        ((vec_rows, state_rows), (za_sig, za_silu), (gate, part, side), (ot, xr, xk, fg), (_, so),
         (v, u, cv, q, zb_sig, zb_silu, yrc)) = overlay(
            [("vec_rows", [P], F32), ("state_rows", [E], F32)],
            [("za_sig", [2, T], F32), ("za_silu", [2, T], F32)],
            [("gate", [2, T], F32), ("part", [2, T], F32), ("side", [D], F32)],
            [("ot", [2, T], F32), ("xr", [2, TT, P], F32), ("xk", [2, TT, P], F32), ("fg", [2, P], F32)],
            [("ot_place", [2, T], F32), ("so", [E], F32)],
            [("v", [T], F32), ("u", [T + 2 * CONV_BUF], F32), ("cv", [2, T + CONV_BUF], F32), ("q", [T], F32),
             ("zb_sig", [T], F32), ("zb_silu", [T], F32), ("yrc", [T], F32)])

        raw = tile("raw", [RING, CW])
        hi = tile("hi", [RING, CW], F32R)
        lo = tile("lo", [RING, CW], F32R)
        ident = tile("ident", [P])
        NVEC = KD + 2 * KD + KE + TAPS * KE
        vec = tile("vec", [NVEC])
        HALO = POOL_BUF + CONV_BUF
        state = tile("state", [KE, HALO])
        carry = tile("carry", [KE, HALO])
        zero = tile("zero", [HALO])
        tails = tile("tails", [KE, 2 * HALO])
        ratio = tile("ratio", [NG, POOL_BUF])
        ssq = tile("ssq", [TT])
        var = tile("var", [TT])
        rstd = tile("rstd", [TT])
        ssq1 = tile("ssq1", [TT])
        var1 = tile("var1", [TT])
        rstd1 = tile("rstd1", [TT])
        sums = tile("sums", [KD, TT])
        ssqy = tile("ssqy", [TT])
        vary = tile("vary", [TT])
        rstdy = tile("rstdy", [TT])
        power = tile("power", [TT])
        spill = nc.dram_tensor("spill", (TT * P, D), F32, kind="Internal").ap()

        ps = [ctx.enter_context(nc.psum_tensor(f"ps{b}", [P, 2, 512], F32)) for b in range(4)]
        flat = [b[:, :, :].rearrange("p b n -> p (b n)") for b in ps]
        cols = [b[:, :, 0:HC] for b in ps]

        def two(a):
            return a.rearrange("p (b n) -> p b n", b=2)

        def f32(a):
            return a.bitcast(F32)

        V_G, V_B, V_S, V_W = 0, KD, 3 * KD, 3 * KD + KE

        def per_channel(c):
            return vec[:, bass.ds(c, 1)]

        raw_landed = [sem(f"raw_landed{s}") for s in range(RING)]
        chunk_hi = sem("chunk_hi")
        chunk_lo = sem("chunk_lo")
        chunk_done = sem("chunk_done")
        drained = [sem(f"drained{b}") for b in range(4)]
        const_set = sem("const_set")
        ident_made = sem("ident_made")
        rows_landed = sem("rows_landed")
        setup_transposed = sem("setup_transposed")
        x_landed = [sem(f"x_landed{t}") for t in range(TT)]
        row_squared = sem("row_squared")
        norm_step = sem("norm_step")
        x_scaled = sem("x_scaled")
        h_turned = sem("h_turned")
        states_turned = sem("states_turned")
        turned_back = sem("turned_back")
        side_landed = sem("side_landed")
        side_step = sem("side_step")
        side_stored = sem("side_stored")
        side_done = sem("side_done")
        xk_landed = [sem(f"xk_landed{e}") for e in range(2)]
        xk_scaled = sem("xk_scaled")
        xr_landed = [sem(f"xr_landed{e}") for e in range(2)]
        spilled = [sem(f"spilled{e}") for e in range(2)]
        sum_step = sem("sum_step")
        sum_made = sem("sum_made")
        h_hi = sem("h_hi")
        mix_landed = sem("mix_landed")
        mix_w_hi = sem("mix_w_hi")
        mix_w_lo = sem("mix_w_lo")
        window_step = sem("window_step")
        diff_made = sem("diff_made")
        diff_hi = sem("diff_hi")
        diff_split = sem("diff_split")
        za_sigmoid = sem("za_sigmoid")
        mix_done = sem("mix_done")
        conv_step = sem("conv_step")
        zb_sigmoid = sem("zb_sigmoid")
        y_raw = sem("y_raw")
        y_hi = sem("y_hi")
        y_split = sem("y_split")
        merged = sem("merged")
        merged_hi = sem("merged_hi")
        merged_split = sem("merged_split")
        res_landed = sem("res_landed")
        y_normed_dve = sem("y_normed_dve")
        y_normed_act = sem("y_normed_act")
        y_stored = sem("y_stored")
        states_stored = sem("states_stored")

        win_v = w_in[0].rearrange("(kh kt p) (b c) -> kh b p kt c", kh=2, p=P, c=P)
        wout_v = w_out[0].rearrange("(kh kt p) (b c) -> kh b p kt c", kh=2, p=P, c=P)
        wpp_v = w_proj_pool[0].rearrange("(kt p) (b c) -> b p kt c", p=P, c=P)
        wpc_v = w_proj_conv[0].rearrange("(kt p) (b c) -> b p kt c", p=P, c=P)
        mix_v = w_pool_mix[0].rearrange("g (kt p) d -> g p kt d", p=P)

        def token_runs(half, prompt, sample):
            out = []
            for first, n in SEGS[half]:
                t = first
                while t < first + n:
                    k = min(P - t % P, first + n - t)
                    if half == 1 and t >= CUT:
                        rows = sample[0, t - CUT:t - CUT + k, :]
                    else:
                        rows = prompt[0, half * T + t:half * T + t + k, :]
                    out.append((t // P, t % P, rows))
                    t += k
            return out

        def x_blocks(half, kt, dst):
            out = []
            for t0, n, src in ((0, T, x_prompt[0, 0:T]),) if half == 0 else \
                    ((0, CUT, x_prompt[0, T:SEQ]), (CUT, T - CUT, x_sample[0])):
                t = 0
                while t < n:
                    tt, p0 = divmod(t0 + t, P)
                    whole = (n - t) // P if p0 == 0 else 0
                    if whole:
                        k = whole * P
                        cols_ = None if dst is None else (
                            dst[:, tt:tt + whole, :],
                            src[t:t + k, bass.ds(kt * P, P)].rearrange("(t p) c -> p t c", p=P))
                    else:
                        k = min(P - p0, n - t)
                        cols_ = None if dst is None else (dst[p0:p0 + k, tt, :], src[t:t + k, bass.ds(kt * P, P)])
                    out.append(cols_)
                    t += k
            return out

        def spill_blocks(e, src):
            full_ = (TT - 1) * P
            return [(spill[0:full_, bass.ds(e * P, P)].rearrange("(t p) c -> p t c", p=P), src[:, 0:TT - 1, :]),
                    (spill[full_:T, bass.ds(e * P, P)], src[0:TL, TT - 1, :])]

        X_RUNS = [token_runs(hf, x_prompt, x_sample) for hf in range(HALVES)]
        Y_RUNS = [token_runs(hf, y_prompt, y_sample) for hf in range(HALVES)]
        XK_DMAS = len(x_blocks(1, 0, None))
        XR_DMAS = len(x_blocks(0, 0, None)) + 1

        def rows_of(tt):
            return P if tt < TT - 1 else TL

        def spans(eng, half, phase, peel_first=False, peel_last=False):
            n = PHASES[phase][0]
            a, b = int(peel_first), n - int(peel_last)
            if peel_first:
                yield 0
            with eng.Fori(a, b) as i:
                yield i
            if peel_last:
                yield n - 1

        def settled(eng, half, phase):
            for b in range(4):
                eng.wait_ge(drained[b], base[f"drained{b}", half, phase])

        block = ctx.enter_context(nc.Block())

        @block.sync
        def _(sp):
            def load(n, k, src, wait=True):
                if wait:
                    sp.wait_ge(chunk_lo, n - RING + 1)
                sp.dma_start(raw[:, k % RING, :].rearrange("p (kt c) -> p kt c", c=P), src) \
                    .then_inc(raw_landed[k % RING], 16)

            for r, src in ((V_G, norm_g[0].rearrange("(r c) -> r c", c=P)),
                           (V_B, b_gate[0].rearrange("(r c) -> r c", c=P)),
                           (V_S, pool_scale[0].rearrange("(r c) -> r c", c=P)),
                           (V_W, w_conv[0].rearrange("w (r c) -> (w r) c", c=P))):
                sp.dma_start(vec_rows[r:r + src.shape[0], :], src).then_inc(rows_landed, 16)
            sp.dma_start(state_rows[0:POOL_BUF, :], state_pool[0, 0]).then_inc(rows_landed, 16)
            sp.dma_start(state_rows[POOL_BUF:HALO, :], state_conv[0, 0]).then_inc(rows_landed, 16)

            sp.wait_ge(x_landed[TT - 2], 16)

            for half in range(HALVES):
                for i in spans(sp, half, "pool", peel_first=half == 0):
                    c0 = at("chunk", half, "pool", i, 0)
                    for k in range(8):
                        blk = (B_XA, B_ZA)[k // 4] + (k // 2) % 2
                        load(c0 + k, k, win_v[k % 2, 2 * i + blk], wait=not (isinstance(i, int) and k < RING))
                        if k == 3:
                            if half == 1:
                                sp.wait_ge(chunk_done, base["chunk", half, "pool"])
                            if not isinstance(i, int):
                                sp.wait_ge(mix_w_lo, at("mix_w_lo", half, "pool", i, 0))
                            sp.dma_start(mix_raw[:, :].rearrange("p (kt d) -> p kt d", d=GROUP), mix_v[i]) \
                                .then_inc(mix_landed, 16)
                for i in spans(sp, half, "mergeA"):
                    c0 = at("chunk", half, "mergeA", i, 0)
                    for k, (ii, r) in enumerate(ROLES):
                        load(c0 + k, k, wpp_v[MU * i + ii] if r == 2 else win_v[r, B_GA + MU * i + ii])
                for i in spans(sp, half, "conv"):
                    c0 = at("chunk", half, "conv", i, 0)
                    for k in range(8):
                        load(c0 + k, k, win_v[k % 2, (B_V, B_CG, B_BG, B_ZB)[k // 2] + i])
                for i in spans(sp, half, "mergeB"):
                    c0 = at("chunk", half, "mergeB", i, 0)
                    for k, (ii, r) in enumerate(ROLES):
                        load(c0 + k, k, wpc_v[MU * i + ii] if r == 2 else win_v[r, B_GB + MU * i + ii])
                out = f"out{half}"
                for i in spans(sp, half, out):
                    c0 = at("chunk", half, out, i, 0)
                    for k in range(4):
                        load(c0 + k, k, wout_v[k % 2, 2 * i + k // 2])
            for tt, p0, rows in Y_RUNS[1]:
                if tt % 2 == 0:
                    sp.wait_ge(y_normed_dve, tt // 2 + 1)
                    sp.dma_start(rows, res[p0:p0 + rows.shape[0], tt, :]).then_inc(y_stored, 16)
            sp.wait_ge(y_stored, 16 * len(Y_RUNS[1]))

        @block.gpsimd
        def _(pool):
            nc.gpsimd.memset(ident[:, :], 0.0).then_inc(ident_made, 1)
            pool.wait_ge(ident_made, 1)
            nc.gpsimd.affine_select(out=ident[:, :], in_=ident[:, :], compare_op=ALU.not_equal, fill=1.0,
                                    base=0, pattern=[[-1, P]], channel_multiplier=1).then_inc(ident_made, 1)
            nc.gpsimd.memset(zero[:, :], 0.0).then_inc(const_set, 1)
            nc.gpsimd.memset(ratio[:, :, :], 1.0).then_inc(const_set, 1)
            pool.wait_ge(const_set, 2)
            for g, w in enumerate(WINDOWS):
                for t in range(w - 1):
                    last = nc.gpsimd.memset(ratio[:, g, t:t + 1], w / (t + 1))
            last.then_inc(const_set, 1)
            nc.gpsimd.memset(power[:, :], -0.5).then_inc(const_set, 1)
            nc.gpsimd.memset(sums[:, :, :], 1.0).then_inc(const_set, 1)
            nc.gpsimd.memset(ssq1[:, :], 1.0).then_inc(const_set, 1)
            pool.wait_ge(const_set, 6)

            def raise_(dst, src, r, c, value):
                pool.wait_ge(norm_step, value)
                nc.gpsimd.tensor_tensor(dst[0:r, c], src[0:r, c], power[0:r, c], ALU.pow).then_inc(norm_step, 1)

            for tt in range(TT):
                raise_(rstd, var, rows_of(tt), slice(tt, tt + 1), at("norm_step", 0, "norm", tt, 1))

            steps, landed = 0, 0
            pool.wait_ge(x_scaled, TT)
            for tt in range(TT):
                r = rows_of(tt)
                if tt > 0:
                    pool.wait_ge(side_step, steps)
                for t, p0, rows in X_RUNS[1]:
                    if t == tt:
                        landed += 16
                        pool.dma_start(side[p0:p0 + rows.shape[0], :], rows).then_inc(side_landed, 16)
                pool.wait_ge(side_landed, landed)
                nc.gpsimd.tensor_tensor(side[0:r, :], side[0:r, :], side[0:r, :], ALU.mult).then_inc(side_step, 1)
                pool.wait_ge(side_step, steps + 1)
                n = D // 2
                k = 1
                while n >= 1:
                    dst = side[0:r, 0:n] if n > 1 else ssq1[0:r, tt:tt + 1]
                    nc.gpsimd.tensor_tensor(dst, side[0:r, 0:n], side[0:r, n:2 * n], ALU.add).then_inc(side_step, 1)
                    k += 1
                    pool.wait_ge(side_step, steps + k)
                    n //= 2
                steps += k
            nc.gpsimd.tensor_scalar(var1[:, :], ssq1[:, :], 1.0 / D, EPS, ALU.mult, ALU.add).then_inc(side_step, 1)
            pool.wait_ge(side_step, steps + 1)
            nc.gpsimd.tensor_tensor(rstd1[:, :], var1[:, :], power[:, :], ALU.pow).then_inc(side_done, 1)

            def load_x(i, e):
                for dst, src in x_blocks(0, 2 * i + e, xr[:, e]):
                    pool.dma_start(dst, src).then_inc(xr_landed[e], 16)
                pool.dma_start(fg[:, e, :], final_norm_g[bass.ds((2 * i + e) * P, P)].rearrange("(a d) -> a d", a=1)
                               .broadcast_to([P, P])).then_inc(xr_landed[e], 16)

            settled(pool, 0, "out0")
            pool.wait_ge(merged, at("merged", 0, "mergeB", PHASES["mergeB"][0], 0))
            for e in range(2):
                load_x(0, e)
            for i in spans(pool, 0, "out0", peel_last=True):
                for e in range(2):
                    pool.wait_ge(sum_made, at("sum_made", 0, "out0", i, e + 1))
                    for dst, src in spill_blocks(2 * i + e, xr[:, e]):
                        pool.dma_start(dst, src).then_inc(spilled[e], 16)
                    if not isinstance(i, int):
                        pool.wait_ge(spilled[e], 32 * i + 32)
                        load_x(i + 1, e)

            raise_(rstdy, vary, P, slice(0, TT), at("norm_step", 0, "final", 0, 2))
            pool.wait_ge(norm_step, at("norm_step", 0, "final", 0, 3))
            for e in range(2):
                pool.wait_ge(spilled[e], 32 * (KD // 2))
            settled(pool, 1, "pool")
            kept, steps = 0, steps + 1
            for tt in range(TT):
                r = rows_of(tt)
                if tt > 0:
                    pool.wait_ge(side_stored, 16 * kept)
                landed += 16
                pool.dma_start(side[0:r, :], spill[tt * P:tt * P + r, :]).then_inc(side_landed, 16)
                pool.wait_ge(side_landed, landed)
                steps += 1
                nc.gpsimd.tensor_scalar(side[0:r, :], side[0:r, :], rstdy[0:r, tt:tt + 1], None, ALU.mult) \
                    .then_inc(side_step, 1)
                pool.wait_ge(side_step, steps)
                for t, p0, rows in Y_RUNS[0]:
                    if t == tt:
                        kept += 1
                        pool.dma_start(rows, side[p0:p0 + rows.shape[0], :]).then_inc(side_stored, 16)
            pool.wait_ge(side_stored, 16 * kept)
            nc.gpsimd.memset(ssq1[:, :], 1.0).then_inc(side_done, 1)

            raise_(rstdy, vary, P, slice(0, TT), at("norm_step", 1, "final", 0, 2))

        @block.tensor
        def _(pe):
            def buffer(b, half, phase, i, use):
                pe.wait_ge(drained[b], at(f"drained{b}", half, phase, i, use))

            def product(b, n, k, rhs, start, stop, each=None, kt0=0):
                pe.wait_ge(chunk_lo, n + 1)
                s = k % RING
                for kt in range(CK):
                    if each is not None:
                        each(kt0 + kt)
                    for w, part in ((hi, 0), (hi, 1), (lo, 0)):
                        for c in range(2):
                            first = start and kt == 0 and w is hi and part == 0
                            last = stop and kt == CK - 1 and w is lo
                            mm = nc.tensor.matmul(ps[b][:, c, 0:HC], w[:, s, kt * P:(kt + 1) * P],
                                                  rhs(kt, part)[:, c * HC:(c + 1) * HC], start=first, stop=last)
                mm.then_inc(chunk_done, 1)

            def full(b, half, phase, i, k, src, each=None):
                n = at("chunk", half, phase, i, k)
                for kh in range(2):
                    product(b, n + kh, k + kh, lambda kt, part: src[:, CK * kh + kt, part, :], kh == 0, kh == 1,
                            each, CK * kh)

            pe.wait_ge(ident_made, 2)
            pe.wait_ge(rows_landed, 96)
            nc.tensor.transpose(flat[0][:, 0:NVEC], vec_rows[0:NVEC, :], ident[0:NVEC, 0:NVEC]) \
                .then_inc(setup_transposed, 1)
            for j in range(KE):
                last = nc.tensor.transpose(flat[1][:, 32 * j:32 * j + HALO], state_rows[0:HALO, j * P:(j + 1) * P],
                                           ident[0:HALO, 0:HALO])
            last.then_inc(setup_transposed, 1)

            def turn(b, src):
                for tt in range(TT):
                    r = rows_of(tt)
                    last = nc.tensor.transpose(flat[b][:, tt * P:tt * P + r], src(tt, r), ident[0:r, 0:r])
                last.then_inc(h_turned, 1)

            def first_turn(kt):
                b = 1 + kt % TURNS
                pe.wait_ge(drained[b], base[f"drained{b}", 0, "prep"] + kt // TURNS)
                turn(b, lambda tt, r: xn[0:r, tt, kt * P:(kt + 1) * P])

            def first_h(kt):
                if 1 <= kt <= KD - TURNS:
                    first_turn(kt + TURNS - 1)
                b = 1 + kt % TURNS
                pe.wait_ge(drained[b], base[f"drained{b}", 0, "prep"] + kt // TURNS + 1)

            pe.wait_ge(x_scaled, TT)
            for kt in range(TURNS):
                first_turn(kt)

            for half in range(HALVES):
                if half == 1:
                    for b in (2, 3):
                        pe.wait_ge(drained[b], base[f"drained{b}", 1, "pool"])

                for i in spans(pe, half, "pool", peel_first=half == 0):
                    for k, b, use in ((0, 0, 0), (2, 1, 0), (4, 2, 0), (6, 0, 1)):
                        first = half == 0 and isinstance(i, int) and k == 0
                        buffer(b, half, "pool", i, use)
                        full(b, half, "pool", i, k, h, first_h if first else None)
                    pe.wait_ge(mix_w_lo, at("mix_w_lo", half, "pool", i, 1))
                    pe.wait_ge(diff_split, at("diff_split", half, "pool", i, 2))
                    for j, b, use in ((0, 1, 1), (1, 3, 0)):
                        buffer(b, half, "pool", i, use)
                        for kt in range(GJ):
                            for w, part in ((mix_hi, 0), (mix_hi, 1), (mix_lo, 0)):
                                for c in range(2):
                                    mm = nc.tensor.matmul(
                                        ps[b][:, c, 0:HC], w[:, kt * GROUP + j * P:kt * GROUP + (j + 1) * P],
                                        ds[:, kt, part, c * HC:(c + 1) * HC],
                                        start=kt == 0 and w is mix_hi and part == 0,
                                        stop=kt == GJ - 1 and w is mix_lo)
                        mm.then_inc(mix_done, 1)

                def merge(phase):
                    def branch(i, ii, k):
                        b = 2 * (ii % 2)
                        if ii == 0:
                            last_y = {"mergeA": ("pool", NG), "mergeB": ("conv", KE)}[phase]
                            pe.wait_ge(y_split, at("y_split", half, *last_y, 0))
                        buffer(b, half, phase, i, ii // 2)
                        product(b, at("chunk", half, phase, i, k), k, lambda kt, part: y[:, kt, part, :],
                                True, True)

                    for i in spans(pe, half, phase):
                        for k, (ii, r) in enumerate(ROLES):
                            if r == 2:
                                branch(i, ii, k)
                            if r == 0:
                                b = 2 * (ii % 2) + 1
                                buffer(b, half, phase, i, ii // 2)
                                full(b, half, phase, i, k, h)

                merge("mergeA")
                for i in spans(pe, half, "conv"):
                    for b in range(4):
                        buffer(b, half, "conv", i, 0)
                        full(b, half, "conv", i, 2 * b, h)
                merge("mergeB")

                out = f"out{half}"

                def back(i, e, use):
                    pe.wait_ge(drained[e], at(f"drained{e}", half, out, i, 1))
                    buffer(2 + e, half, out, i, use)
                    for tt in range(TT):
                        r = rows_of(tt)
                        last = nc.tensor.transpose(flat[2 + e][0:r, tt * P:(tt + 1) * P],
                                                   ot[:, e, tt * P:tt * P + r], ident[:, :])
                    last.then_inc(turned_back, 1)

                def next_h(i, e):
                    if half == 0:
                        pe.wait_ge(xk_scaled, at("xk_scaled", 0, out, i, e + 1))
                        buffer(2 + e, 0, out, i, 0)
                        turn(2 + e, lambda tt, r: xk[0:r, e, tt, :])

                def new_states():
                    pe.wait_ge(zb_sigmoid, at("zb_sigmoid", half, "conv", KE, 0))
                    buffer(3, half, "state", 0, 0)
                    for j in range(KE):
                        last = nc.tensor.transpose(flat[3][0:2 * HALO, j * P:(j + 1) * P], tails[:, j, :],
                                                   ident[:, :])
                    last.then_inc(states_turned, 1)

                behind = 2 if half == 0 else 1
                for i in spans(pe, half, out, peel_first=True):
                    first = isinstance(i, int)
                    each = None
                    if first:
                        each = lambda kt: pe.wait_ge(merged_split, at("merged_split", half, "split", kt, 1))
                    for k in range(4):
                        if k % 2 == 0:
                            buffer(k // 2, half, out, i, 0)
                        product(k // 2, at("chunk", half, out, i, k), k,
                                lambda kt, part: ms[:, CK * (k % 2) + kt, part, :], k % 2 == 0, k % 2 == 1,
                                each if k < 2 else None, CK * (k % 2))
                        if k == 0 and not first:
                            back(i - 1, 1, behind - 1)
                        if k == 0 and first and half == 1:
                            new_states()
                        if k == 2:
                            back(i, 0, behind - 1)
                        if k % 2 == 1:
                            next_h(i, k // 2)
                back(PHASES[out][0] - 1, 1, behind - 1)

        @block.scalar
        def _(act):
            def ahead(half, phase, i, k):
                n = at("chunk", half, phase, i, k)
                act.wait_ge(chunk_done, n + 1)
                s = k % RING
                act.wait_ge(raw_landed[s], (16 // RING) * (n - s) + 32)
                nc.scalar.activation(hi[:, s, :], raw[:, s, :], ACT.Copy).then_inc(chunk_hi, 1)

            def done(half, phase, i, k):
                act.wait_ge(chunk_done, at("chunk", half, phase, i, k) + 1)

            def first_split(s):
                act.wait_ge(raw_landed[s], 16)
                nc.scalar.activation(hi[:, s, :], raw[:, s, :], ACT.Copy).then_inc(chunk_hi, 1)

            for tt, p0, rows in X_RUNS[0]:
                act.dma_start(xn[p0:p0 + rows.shape[0], tt, :], rows).then_inc(x_landed[tt], 16)
            for tt in range(TT):
                r = rows_of(tt)
                act.wait_ge(x_landed[tt], 16)
                if tt > 0:
                    act.wait_ge(row_squared, tt)
                nc.scalar.activation(junk[0:r, :], xn[0:r, tt, :], ACT.Square,
                                     accum_out=ssq[0:r, tt:tt + 1]).then_inc(row_squared, 1)
            act.wait_ge(const_set, 6)
            for b in range(2):
                act.wait_ge(drained[b], 1)
            for kt in range(KD):
                if kt % 4 == 0:
                    first_split(kt // 4)
                b = 1 + kt % TURNS
                act.wait_ge(h_turned, kt + 1)
                nc.scalar.activation(h[:, kt, 0, :], flat[b][:, 0:T], ACT.Copy,
                                     scale=per_channel(V_G + kt)).then_inc(h_hi, 1)

            for half in range(HALVES):
                settled(act, half, "pool")
                for i in spans(act, half, "pool"):
                    for k in range(8):
                        ahead(half, "pool", i, k)
                        if k == 4:
                            act.wait_ge(mix_landed, at("mix_landed", half, "pool", i, 16))
                            nc.scalar.activation(mix_hi[:, :], mix_raw[:, :], ACT.Copy).then_inc(mix_w_hi, 1)
                        if k in (1, 3):
                            j = k // 2
                            act.wait_ge(diff_made, at("diff_made", half, "pool", i, j + 1 - 2))
                            jb = 2 * i + j
                            left = zero[:, 0:POOL_BUF] if half == 0 else carry[:, jb, 0:POOL_BUF]
                            nc.scalar.copy(xe[:, j, 0:POOL_BUF], left)
                            if half == 1:
                                c = ext(1, CUT, POOL_BUF) - POOL_BUF
                                nc.scalar.copy(xe[:, j, c:c + POOL_BUF], state[:, jb, 0:POOL_BUF])
                            for s, (first, n) in enumerate(SEGS[half]):
                                c = first + n - POOL_BUF - HC
                                dst = carry[:, jb, 0:POOL_BUF] if half == 0 else \
                                    tails[:, jb, s * POOL_BUF:(s + 1) * POOL_BUF]
                                nc.scalar.copy(dst, ps[j][:, 1, c:c + POOL_BUF])
                            for bank, c, first, n in PIECES[half]:
                                e0 = ext(half, first, POOL_BUF)
                                last = nc.scalar.copy(xe[:, j, e0:e0 + n], ps[j][:, bank, c:c + n])
                            last.then_inc(drained[j], 1)
                        if k in (2, 4):
                            j = k // 2 - 1
                            act.wait_ge(diff_made, at("diff_made", half, "pool", i, j + 1))
                            nc.scalar.copy(ds[:, j, 0, :], dr[:, j, :]).then_inc(diff_hi, 1)
                        if k in (5, 7):
                            j = (k - 5) // 2
                            nc.scalar.activation(two(za_sig[:, j, :]), cols[(2, 0)[j]], ACT.Sigmoid) \
                                .then_inc(za_sigmoid, 1)
                    for j, b, use in ((0, 1, 2), (1, 3, 1)):
                        act.wait_ge(drained[b], at(f"drained{b}", half, "pool", i, use))
                        nc.scalar.copy(y[:, 2 * i + j, 0, :], yrp[:, j, :]).then_inc(y_hi, 1)

                def merged_split_hi(s):
                    if 2 * s >= KD:
                        act.wait_ge(merged_split, at("merged_split", half, "split", 2 * s - KD, 1))
                    nc.scalar.copy(ms[:, s, 0, :], m[:, s, :]).then_inc(merged_hi, 1)

                def merge(phase, bias0, peel_last=False):
                    settled(act, half, phase)
                    for i in spans(act, half, phase, peel_last=peel_last):
                        for k in range(3 * MU):
                            ahead(half, phase, i, k)
                            if peel_last and isinstance(i, int) and k in (3 * MU - 3, 3 * MU - 2):
                                act.wait_ge(merged, at("merged", half, phase, i, MU - 1))
                                n = EARLY // 2
                                s0 = 0 if k == 3 * MU - 3 else n
                                for s in range(s0, s0 + n):
                                    merged_split_hi(s)
                            if k % 3 == 2:
                                ii = k // 3
                                g = ii % 2
                                nc.scalar.activation(two(gate[:, g, :]), cols[2 * g + 1], ACT.Sigmoid,
                                                     bias=per_channel(bias0 + MU * i + ii)) \
                                    .then_inc(drained[2 * g + 1], 1)

                merge("mergeA", V_B)

                settled(act, half, "conv")
                act.wait_ge(side_done, half + 1)
                for i in spans(act, half, "conv"):
                    for k in range(8):
                        ahead(half, "conv", i, k)
                        if k == 1:
                            left = zero[:, 0:CONV_BUF] if half == 0 else carry[:, i, POOL_BUF:HALO]
                            nc.scalar.copy(u[:, 0:CONV_BUF], left)
                            if half == 1:
                                c = ext(1, CUT, CONV_BUF) - CONV_BUF
                                nc.scalar.copy(u[:, c:c + CONV_BUF], state[:, i, POOL_BUF:HALO])
                            nc.scalar.copy(two(v[:, :]), cols[0]).then_inc(drained[0], 1)
                        if k == 4:
                            act.wait_ge(drained[1], at("drained1", half, "conv", i, 1))
                            for s, (first, n) in enumerate(SEGS[half]):
                                c = ext(half, first + n - 1, CONV_BUF) + 1 - CONV_BUF
                                d0 = 2 * POOL_BUF + s * CONV_BUF
                                dst = carry[:, i, POOL_BUF:HALO] if half == 0 else tails[:, i, d0:d0 + CONV_BUF]
                                nc.scalar.copy(dst, u[:, c:c + CONV_BUF])
                        if k == 7:
                            nc.scalar.activation(two(zb_sig[:, :]), cols[3], ACT.Sigmoid).then_inc(zb_sigmoid, 1)
                    act.wait_ge(y_raw, at("y_raw", half, "conv", i, 1))
                    nc.scalar.copy(y[:, i, 0, :], yrc[:, :]).then_inc(y_hi, 1)

                merge("mergeB", V_B + KD, peel_last=True)
                act.wait_ge(merged, at("merged", half, "mergeB", PHASES["mergeB"][0], 0))
                for s in range(EARLY, KD):
                    merged_split_hi(s)

                out = f"out{half}"
                for b in range(4):
                    act.wait_ge(drained[b], base[f"drained{b}", half, "state" if (half, b) == (1, 3) else out])
                if half == 1:
                    for tt, p0, rows in X_RUNS[1]:
                        act.dma_start(res[p0:p0 + rows.shape[0], tt, :], rows).then_inc(res_landed, 16)
                    act.dma_start(fin_g[:, :], final_norm_g.rearrange("(a d) -> a d", a=1)
                                  .broadcast_to([P, D])).then_inc(res_landed, 16)

                def store_states():
                    act.wait_ge(drained[3], at("drained3", half, "state", 0, 1))
                    r = 0
                    for dst in (new_pool_prompt, new_pool_sample, new_conv_prompt, new_conv_sample):
                        n = dst.shape[2]
                        act.dma_start(dst[0, 0], so[r:r + n, :]).then_inc(states_stored, 16)
                        r += n

                def load_xk(i, e):
                    for dst, src in x_blocks(1, 2 * i + e, xk[:, e]):
                        act.dma_start(dst, src).then_inc(xk_landed[e], 16)

                def next_h_hi(i, e):
                    act.wait_ge(h_turned, at("h_turned", 0, out, i, e + 1))
                    nc.scalar.activation(h[:, 2 * i + e, 0, :], flat[2 + e][:, 0:T], ACT.Copy,
                                         scale=per_channel(V_G + 2 * i + e)).then_inc(h_hi, 1)

                if half == 0:
                    for e in range(2):
                        load_xk(0, e)
                for i in spans(act, half, out, peel_last=True):
                    for k in range(4):
                        if half == 1 and isinstance(i, int):
                            done(half, out, i, k)
                        else:
                            ahead(half, out, i, k)
                        if half == 1 and isinstance(i, int) and k == 0:
                            store_states()
                        if k % 2 == 1:
                            e = k // 2
                            nc.scalar.copy(two(ot[:, e, :]), cols[e]).then_inc(drained[e], 1)
                            if half == 0:
                                next_h_hi(i, e)
                                if not isinstance(i, int):
                                    load_xk(i + 1, e)

            act.wait_ge(norm_step, at("norm_step", 1, "final", 0, 3))
            act.wait_ge(sum_made, at("sum_made", 1, "out1", PHASES["out1"][0], 0))
            n = 0
            for tt in range(1, TT, 2):
                nc.scalar.activation(res[:, tt, :], res[:, tt, :], ACT.Copy, scale=rstdy[:, tt:tt + 1]) \
                    .then_inc(y_normed_act, 1)
                n += 1
                act.wait_ge(y_normed_act, n)
                for t, p0, rows in Y_RUNS[1]:
                    if t == tt:
                        act.dma_start(rows, res[p0:p0 + rows.shape[0], tt, :]).then_inc(y_stored, 16)
            act.wait_ge(states_stored, 64)
            act.wait_ge(y_stored, 16 * len(Y_RUNS[1]))

        @block.vector
        def _(dve):
            def split(n, s):
                dve.wait_ge(chunk_hi, n + 1)
                nc.vector.tensor_tensor(lo[:, s, :], raw[:, s, :], f32(hi[:, s, :]), ALU.subtract) \
                    .then_inc(chunk_lo, 1)

            def ahead(half, phase, i, k):
                split(at("chunk", half, phase, i, k) + RING, k % RING)

            def y_lo(half, phase, i, k, jb, src):
                dve.wait_ge(y_hi, at("y_hi", half, phase, i, k))
                nc.vector.tensor_tensor(y[:, jb, 1, :], src, f32(y[:, jb, 0, :]), ALU.subtract) \
                    .then_inc(y_split, 1)

            steps = [0]

            def window_link(ins):
                steps[0] += 1
                ins.then_inc(window_step, 1)
                dve.wait_ge(window_step, steps[0])

            nc.vector.memset(var[:, :], 0.0).then_inc(diff_made, 2)
            dve.wait_ge(const_set, 6)
            dve.wait_ge(diff_made, 2)

            for tt in range(TT):
                r = rows_of(tt)
                if tt == TT - 1:
                    dve.wait_ge(setup_transposed, 1)
                    nc.vector.tensor_copy(vec[:, :], flat[0][:, 0:NVEC]).then_inc(drained[0], 1)
                    dve.wait_ge(setup_transposed, 2)
                    nc.vector.tensor_copy(state[:, :, :], flat[1][:, 0:32 * KE].rearrange(
                        "p (j n) -> p j n", n=32)[:, :, 0:HALO]).then_inc(drained[1], 1)
                    for b in range(2):
                        dve.wait_ge(drained[b], 1)
                dve.wait_ge(row_squared, tt + 1)
                nc.vector.tensor_scalar(var[0:r, tt:tt + 1], ssq[0:r, tt:tt + 1], 1.0 / D, EPS, ALU.mult, ALU.add) \
                    .then_inc(norm_step, 1)
                dve.wait_ge(norm_step, at("norm_step", 0, "norm", tt, 2))
                nc.vector.tensor_scalar(xn[0:r, tt, :], xn[0:r, tt, :], rstd[0:r, tt:tt + 1], None, ALU.mult) \
                    .then_inc(x_scaled, 1)

            def h_lo(kt, b, value):
                dve.wait_ge(h_hi, value)
                nc.vector.scalar_tensor_tensor(h[:, kt, 1, :], flat[b][:, 0:T], per_channel(V_G + kt),
                                               f32(h[:, kt, 0, :]), ALU.mult, ALU.subtract) \
                    .then_inc(drained[b], 1)

            for kt in range(KD):
                if kt % 4 == 0:
                    split(kt // 4, kt // 4)
                h_lo(kt, 1 + kt % TURNS, kt + 1)

            for half in range(HALVES):
                for g, w in enumerate(WINDOWS):
                    for k in range(8):
                        ahead(half, "pool", g, k)
                        if k == 4:
                            dve.wait_ge(mix_w_hi, at("mix_w_hi", half, "pool", g, 1))
                            nc.vector.tensor_tensor(mix_lo[:, :], mix_raw[:, :], f32(mix_hi[:, :]), ALU.subtract) \
                                .then_inc(mix_w_lo, 1)
                        if k in (1, 3):
                            j = k // 2
                            width = ext(half, T - 1, POOL_BUF) + 1
                            dve.wait_ge(drained[j], at(f"drained{j}", half, "pool", g, 1))
                            src, reach, n = xe[:, j, :], 0, 1
                            while n < w:
                                dst = ws[:, n.bit_length() % 2, :]
                                lo_c = reach + n
                                window_link(nc.vector.tensor_tensor(
                                    dst[:, lo_c:width], src[:, lo_c:width], src[:, lo_c - n:width - n], ALU.add))
                                src, reach, n = dst, lo_c, 2 * n
                            if half == 0:
                                s0 = src[:, POOL_BUF:2 * POOL_BUF]
                                window_link(nc.vector.tensor_tensor(s0, s0, ratio[:, g, :], ALU.mult))
                            for first, n in SEGS[half]:
                                e0 = ext(half, first, POOL_BUF)
                                last = nc.vector.scalar_tensor_tensor(
                                    dr[:, j, first:first + n], src[:, e0:e0 + n], 1.0 / w, xe[:, j, e0:e0 + n],
                                    ALU.mult, ALU.subtract)
                            last.then_inc(diff_made, 1)
                        if k in (2, 4):
                            j = k // 2 - 1
                            dve.wait_ge(diff_hi, at("diff_hi", half, "pool", g, j + 1))
                            nc.vector.tensor_tensor(ds[:, j, 1, :], dr[:, j, :], f32(ds[:, j, 0, :]), ALU.subtract) \
                                .then_inc(diff_split, 1)
                        if k in (5, 7):
                            j = (k - 5) // 2
                            dve.wait_ge(za_sigmoid, at("za_sigmoid", half, "pool", g, j + 1))
                            b = (2, 0)[j]
                            if half == 1 and g == 0 and j == 0:
                                for e in range(2):
                                    dve.wait_ge(spilled[e], 32 * (KD // 2))
                            nc.vector.tensor_tensor(two(za_silu[:, j, :]), cols[b], two(za_sig[:, j, :]),
                                                    ALU.mult).then_inc(drained[b], 1)
                    for j, b, za, use in ((0, 1, 2, 1), (1, 3, 0, 2)):
                        dve.wait_ge(mix_done, at("mix_done", half, "pool", g, j + 1))
                        dve.wait_ge(drained[za], at(f"drained{za}", half, "pool", g, use))
                        nc.vector.scalar_tensor_tensor(two(yrp[:, j, :]), cols[b], per_channel(V_S + 2 * g + j),
                                                       two(za_silu[:, j, :]), ALU.mult, ALU.mult) \
                            .then_inc(drained[b], 1)
                    for j in range(GJ):
                        y_lo(half, "pool", g, j + 1, 2 * g + j, yrp[:, j, :])

                for i in spans(dve, half, "mergeA"):
                    for k in range(3 * MU):
                        ahead(half, "mergeA", i, k)
                        if k % 3 == 2:
                            ii = k // 3
                            b = 2 * (ii % 2)
                            dve.wait_ge(drained[b + 1], at(f"drained{b + 1}", half, "mergeA", i, ii // 2 + 1))
                            nc.vector.tensor_tensor(two(m[:, MU * i + ii, :]), cols[b], two(gate[:, ii % 2, :]),
                                                    ALU.mult).then_inc(drained[b], 1)

                dve.wait_ge(side_done, half + 1)
                for i in spans(dve, half, "conv"):
                    width = ext(half, T - 1, CONV_BUF) + 1 - CONV_BUF
                    for k in range(8):
                        ahead(half, "conv", i, k)
                        if k == 3:
                            dve.wait_ge(drained[0], at("drained0", half, "conv", i, 1))
                            for bank, c, first, n in PIECES[half]:
                                e0 = ext(half, first, CONV_BUF)
                                last = nc.vector.tensor_tensor(u[:, e0:e0 + n], ps[1][:, bank, c:c + n],
                                                               v[:, first:first + n], ALU.mult)
                            last.then_inc(drained[1], 1)
                            dve.wait_ge(drained[1], at("drained1", half, "conv", i, 1))
                            tap = [per_channel(V_W + KE * w + i) for w in range(TAPS)]
                            nc.vector.tensor_scalar(cv[:, 0, 0:width], u[:, 0:width], tap[0], None, ALU.mult) \
                                .then_inc(conv_step, 1)
                            for w in range(1, TAPS):
                                dve.wait_ge(conv_step, at("conv_step", half, "conv", i, w))
                                nc.vector.scalar_tensor_tensor(cv[:, w % 2, 0:width], u[:, w:w + width], tap[w],
                                                               cv[:, (w - 1) % 2, 0:width], ALU.mult, ALU.add) \
                                    .then_inc(conv_step, 1)
                        if k == 5:
                            dve.wait_ge(conv_step, at("conv_step", half, "conv", i, TAPS))
                            for bank, c, first, n in PIECES[half]:
                                e0 = ext(half, first, CONV_BUF) - CONV_BUF
                                last = nc.vector.tensor_tensor(q[:, first:first + n], ps[2][:, bank, c:c + n],
                                                               cv[:, (TAPS - 1) % 2, e0:e0 + n], ALU.mult)
                            last.then_inc(drained[2], 1)
                        if k == 7:
                            dve.wait_ge(zb_sigmoid, at("zb_sigmoid", half, "conv", i, 1))
                            nc.vector.tensor_tensor(two(zb_silu[:, :]), cols[3], two(zb_sig[:, :]), ALU.mult) \
                                .then_inc(drained[3], 1)
                            for b in (2, 3):
                                dve.wait_ge(drained[b], at(f"drained{b}", half, "conv", i, 1))
                            nc.vector.tensor_tensor(yrc[:, :], q[:, :], zb_silu[:, :], ALU.mult).then_inc(y_raw, 1)
                    y_lo(half, "conv", i, 1, i, yrc[:, :])

                def merged_split_lo(s):
                    dve.wait_ge(merged_hi, at("merged_hi", half, "split", s, 1))
                    if 2 * s >= KD:
                        dve.wait_ge(merged_split, at("merged_split", half, "split", min(2 * s - KD + 1, s - 1), 1))
                    nc.vector.tensor_tensor(ms[:, s, 1, :], m[:, s, :], f32(ms[:, s, 0, :]), ALU.subtract) \
                        .then_inc(merged_split, 1)

                for i in spans(dve, half, "mergeB", peel_last=True):
                    for k in range(3 * MU):
                        ahead(half, "mergeB", i, k)
                        if isinstance(i, int) and k in (3 * MU - 3, 3 * MU - 2):
                            n = EARLY // 2
                            s0 = 0 if k == 3 * MU - 3 else n
                            for s in range(s0, s0 + n):
                                merged_split_lo(s)
                        if k % 3 == 2:
                            ii = k // 3
                            b = 2 * (ii % 2)
                            dve.wait_ge(drained[b + 1], at(f"drained{b + 1}", half, "mergeB", i, ii // 2 + 1))
                            nc.vector.tensor_tensor(two(part[:, ii % 2, :]), cols[b], two(gate[:, ii % 2, :]),
                                                    ALU.mult).then_inc(drained[b], 1)
                            dve.wait_ge(drained[b], at(f"drained{b}", half, "mergeB", i, ii // 2 + 1))
                            mb = m[:, MU * i + ii, :]
                            nc.vector.tensor_tensor(mb, mb, part[:, ii % 2, :], ALU.add).then_inc(merged, 1)

                for s in range(EARLY, KD):
                    merged_split_lo(s)
                out = f"out{half}"

                def sum_block(i, e):
                    eb = 2 * i + e
                    dve.wait_ge(turned_back, at("turned_back", half, out, i, e + 1))
                    if half == 0:
                        dve.wait_ge(xr_landed[e], 16 * XR_DMAS * i + 16 * XR_DMAS)
                        a = xr[:, e, 0:TT - 1, :], xr[0:TL, e, TT - 1, :]
                        g = fg[:, e, :]
                    else:
                        a = res[:, 0:TT - 1, bass.ds(eb * P, P)], res[0:TL, TT - 1, bass.ds(eb * P, P)]
                        g = fin_g[:, bass.ds(eb * P, P)]
                    o = (flat[2 + e][:, 0:(TT - 1) * P].rearrange("p (t n) -> p t n", n=P),
                         flat[2 + e][0:TL, (TT - 1) * P:TT * P])
                    n0 = at("sum_step", half, out, i, 2 * e)
                    nc.vector.tensor_tensor(a[0], a[0], o[0], ALU.add)
                    nc.vector.tensor_tensor(a[1], a[1], o[1], ALU.add).then_inc(sum_step, 1)
                    dve.wait_ge(sum_step, n0 + 1)
                    nc.vector.tensor_tensor(o[0], a[0], a[0], ALU.mult)
                    nc.vector.tensor_tensor(o[1], a[1], a[1], ALU.mult).then_inc(sum_step, 1)
                    dve.wait_ge(sum_step, n0 + 2)
                    nc.vector.reduce_sum(sums[:, eb, 0:TT - 1], o[0], mybir.AxisListType.X)
                    nc.vector.reduce_sum(sums[0:TL, eb, TT - 1:TT], o[1], mybir.AxisListType.X) \
                        .then_inc(drained[2 + e], 1)

                    def times_g():
                        gb = g.rearrange("p (a n) -> p a n", a=1).broadcast_to([P, TT - 1, P])
                        nc.vector.tensor_tensor(a[0], a[0], gb, ALU.mult)
                        nc.vector.tensor_tensor(a[1], a[1], g[0:TL], ALU.mult).then_inc(sum_made, 1)
                    return times_g

                def scale_xk(i, e):
                    dve.wait_ge(xk_landed[e], 16 * XK_DMAS * i + 16 * XK_DMAS)
                    a = xk[:, e, 0:TT - 1, :]
                    nc.vector.tensor_tensor(a, a, rstd1[:, 0:TT - 1].rearrange("p (t a) -> p t a", a=1)
                                            .broadcast_to([P, TT - 1, P]), ALU.mult)
                    a = xk[0:TL, e, TT - 1, :]
                    nc.vector.tensor_scalar(a, a, rstd1[0:TL, TT - 1:TT], None, ALU.mult).then_inc(xk_scaled, 1)

                def next_h_lo(i, e):
                    h_lo(2 * i + e, 2 + e, at("h_hi", 0, out, i, e + 1))

                if half == 0:
                    scale_xk(0, 0)
                else:
                    dve.wait_ge(res_landed, 16 * (len(X_RUNS[1]) + 1))
                for i in spans(dve, half, out, peel_first=True, peel_last=True):
                    first = isinstance(i, int) and i == 0
                    last_i = isinstance(i, int) and i > 0
                    for k in range(4):
                        if not (half == 1 and last_i):
                            ahead(half, out, i, k)
                        if k == 0 and first and half == 1:
                            dve.wait_ge(states_turned, 1)
                            nc.vector.tensor_copy(so[0:2 * HALO, :], flat[3][0:2 * HALO, 0:E]) \
                                .then_inc(drained[3], 1)
                        if k == 0 and not first:
                            sum_block(i - 1, 1)()
                        if k == 2:
                            sum_block(i, 0)()
                        if half == 0 and k == 1:
                            next_h_lo(i, 0)
                            scale_xk(i, 1)
                        if half == 0 and k == 3:
                            next_h_lo(i, 1)
                            if not last_i:
                                scale_xk(i + 1, 0)
                last_times_g = sum_block(PHASES[out][0] - 1, 1)
                for b in (2, 3):
                    dve.wait_ge(drained[b], count[f"drained{b}"] if half == 1 else base[f"drained{b}", 1, "pool"])
                nc.vector.reduce_sum(ssqy[:, :], sums[:, :, :].rearrange("p e t -> p t e"), mybir.AxisListType.X) \
                    .then_inc(norm_step, 1)
                dve.wait_ge(norm_step, at("norm_step", half, "final", 0, 1))
                nc.vector.tensor_scalar(vary[:, :], ssqy[:, :], 1.0 / D, EPS, ALU.mult, ALU.add) \
                    .then_inc(norm_step, 1)
                last_times_g()
            dve.wait_ge(norm_step, at("norm_step", 1, "final", 0, 3))
            dve.wait_ge(sum_made, at("sum_made", 1, "out1", PHASES["out1"][0], 0))
            for tt in range(0, TT, 2):
                r = rows_of(tt)
                nc.vector.tensor_scalar(res[0:r, tt, :], res[0:r, tt, :], rstdy[0:r, tt:tt + 1], None, ALU.mult) \
                    .then_inc(y_normed_dve, 1)


_INS = ['x_prompt', 'x_sample', 'state_pool', 'state_conv', 'norm_g', 'w_in', 'b_gate', 'w_pool_mix',
        'pool_scale', 'w_conv', 'w_proj_pool', 'w_proj_conv', 'w_out', 'final_norm_g']


def kernel(**inputs):
    import numpy as _np
    import concourse.bacc as _bacc
    from concourse import mybir as _mybir
    from concourse.bass_utils import run_bass_kernel_spmd as _run

    nc = _bacc.Bacc("TRN2", target_bir_lowering=False, num_devices=1)
    arrays, args = {}, []
    for name in _INS:
        a = _np.ascontiguousarray(inputs[name])
        arrays[f"in_{name}_dram"] = a
        args.append(nc.dram_tensor(f"in_{name}_dram", a.shape, _mybir.dt.from_np(a.dtype), kind="ExternalInput").ap())
    depth, _, pool_buf, e_pool = inputs['state_pool'].shape
    conv_buf, e_conv = inputs['state_conv'].shape[2:]
    b, db = inputs['x_prompt'].shape[0], inputs['x_sample'].shape[0]
    outs = [inputs['x_prompt'].shape, inputs['x_sample'].shape, (depth, b, pool_buf, e_pool),
            (depth, b, conv_buf, e_conv), (depth, db, pool_buf, e_pool), (depth, db, conv_buf, e_conv)]
    for i, shape in enumerate(outs):
        args.append(nc.dram_tensor(f"out_{i}_dram", tuple(shape), _mybir.dt.float32, kind="ExternalOutput").ap())
    bass_hybrid_stream_step(nc, *args)
    r = _run(nc, [arrays], core_ids=[0])
    return tuple(r.results[0][f"out_{i}_dram"] for i in range(len(outs)))
```

```python
from contextlib import ExitStack

import concourse.bass as bass
from concourse import mybir

F32 = mybir.dt.float32
F32R = mybir.dt.float32r
ALU = mybir.AluOpType
ACT = mybir.ActivationFunctionType

P = 128
HALVES = 2
RING = 4
EPS = 1e-6
WINDOWS = (2, 4, 8, 16)


def bass_hybrid_stream_step(nc, x_prompt, x_sample, state_pool, state_conv, norm_g, w_in, b_gate,
                            w_pool_mix, pool_scale, w_conv, w_proj_pool, w_proj_conv, w_out,
                            final_norm_g, y_prompt, y_sample, new_pool_prompt, new_conv_prompt,
                            new_pool_sample, new_conv_sample):
    _, SEQ, D = x_prompt.shape
    DEC = x_sample.shape[1]
    E = w_proj_pool.shape[1]
    POOL_BUF = state_pool.shape[2]
    CONV_BUF = state_conv.shape[2]
    TAPS = w_conv.shape[1]
    GROUP = w_pool_mix.shape[2]

    T = (SEQ + DEC) // HALVES
    HC = T // 2
    KD = D // P
    KE = E // P
    CK = 8
    CW = CK * P
    GJ = GROUP // P
    NG = E // GROUP
    TT = -(-T // P)
    TL = T - (TT - 1) * P
    FT = HC // P
    CUT = SEQ - T
    MU = 4
    assert KD == 2 * CK and KE == CK and NG == len(WINDOWS) and KD % MU == 0 and GJ == 2

    SEGS = [[(0, T)], [(0, CUT), (CUT, T - CUT)]]
    PIECES = [[(0, 0, 0, HC), (1, 0, HC, HC)],
              [(0, 0, 0, HC), (1, 0, HC, CUT - HC), (1, CUT - HC, CUT, T - CUT)]]

    def ext(half, t, halo):
        return halo + t + (halo if half == 1 and t >= CUT else 0)

    B_XA, B_ZA, B_V, B_BG, B_CG, B_ZB = (k * KE for k in range(6))
    B_GA = 6 * KE
    B_GB = B_GA + KD

    ROLES = [(ii, r) for ii in range(MU) for r in ((0, 1, 2) if ii < MU - 1 else (2, 0, 1))]
    EARLY = KD // 2

    one_each = {f"drained{b}": 1 for b in range(4)}
    two_each = {f"drained{b}": 2 for b in range(4)}
    PHASES = {
        "setup": (1, {"drained0": 2, "diff_made": 2}),
        "norm": (TT, {"row_squared": 1, "norm_step": 2, "x_scaled": 1}),
        "prep": (KD, {"h_turned": 1, "h_hi": 1}),
        "pool": (NG, {"chunk": 8, **one_each, "drained0": 2, "drained1": 2, "mix_landed": 16,
                      "mix_w_hi": 1, "mix_w_lo": 1, "diff_made": 2, "diff_hi": 2, "diff_split": 2,
                      "za_sigmoid": 2, "mix_done": 2, "y_hi": 2, "y_split": 2}),
        "mergeA": (KD // MU, {"chunk": 3 * MU, **two_each}),
        "conv": (KE, {"chunk": 8, **one_each, "conv_step": TAPS, "zb_sigmoid": 1, "y_raw": 1,
                      "y_hi": 1, "y_split": 1}),
        "mergeB": (KD // MU, {"chunk": 3 * MU, **two_each, "merged": MU}),
        "state": (1, {"drained3": 1, "states_turned": 1}),
        "split": (KD, {"merged_hi": 1, "merged_split": 1}),
        "out0": (KD // 2, {"chunk": 4, "drained0": 1, "drained1": 1, "drained2": 2, "drained3": 2,
                           "turned_back": 2, "sum_step": 4, "sum_made": 2, "h_turned": 2, "h_hi": 2,
                           "xk_scaled": 2}),
        "out1": (KD // 2, {"chunk": 4, **one_each, "turned_back": 2, "sum_step": 4, "sum_made": 2}),
        "final": (1, {"norm_step": 3}),
    }
    COURSE = [[(0, p) for p in ("setup", "norm", "prep", "pool", "mergeA", "conv", "mergeB", "split",
                                "out0", "final")],
              [(1, p) for p in ("pool", "mergeA", "conv", "mergeB", "state", "split", "out1", "final")]]
    TURNS = 3
    base, count = {}, {}
    for half, phase in COURSE[0] + COURSE[1]:
        n, ticks = PHASES[phase]
        for s, k in ticks.items():
            base[s, half, phase] = count.get(s, 0)
            count[s] = count.get(s, 0) + n * k
        if phase == "prep":
            for b in range(TURNS):
                s = f"drained{1 + b}"
                base[s, half, phase] = count.get(s, 0)
                count[s] = count.get(s, 0) + len(range(b, KD, TURNS))

    def at(s, half, phase, i, k):
        return base[s, half, phase] + PHASES[phase][1][s] * i + k

    with ExitStack() as ctx:
        def sem(name):
            return ctx.enter_context(nc.semaphore(name))

        def tile(name, shape, dt=F32):
            return ctx.enter_context(nc.sbuf_tensor(name, [P, *shape], dt))

        def overlay(*groups):
            out = []
            for group in groups[:-1]:
                with ExitStack() as s:
                    out.append([s.enter_context(nc.sbuf_tensor(n, [P, *shape], dt))
                                for n, shape, dt in group])
            out.append([tile(*t) for t in groups[-1]])
            return out

        (res, fin_g), (junk,), (h,) = overlay(
            [("res", [TT, D], F32), ("fin_g", [D], F32)],
            [("junk", [D], F32)],
            [("h", [KD, 2, T], F32R)])
        ((xn,), (y, xe, ws, dr, ds, yrp, mix_raw, mix_hi, mix_lo), (_, m), (ms,)) = overlay(
            [("xn", [TT, D], F32)],
            [("y", [KE, 2, T], F32R), ("xe", [2, T + 2 * POOL_BUF], F32), ("ws", [2, T + 2 * POOL_BUF], F32),
             ("dr", [2, T], F32), ("ds", [2, 2, T], F32R), ("yrp", [2, T], F32),
             ("mix_raw", [GJ * GROUP], F32), ("mix_hi", [GJ * GROUP], F32R), ("mix_lo", [GJ * GROUP], F32R)],
            [("y_place", [KE, 2, T], F32R), ("m", [KD, T], F32)],
            [("ms", [KD, 2, T], F32R)])
        ((vec_rows, state_rows), (za_sig, za_silu), (gate, part, side), (ot, xr, xk, fg), (_, so),
         (v, u, cv, q, zb_sig, zb_silu, yrc)) = overlay(
            [("vec_rows", [P], F32), ("state_rows", [E], F32)],
            [("za_sig", [2, T], F32), ("za_silu", [2, T], F32)],
            [("gate", [2, T], F32), ("part", [2, T], F32), ("side", [D], F32)],
            [("ot", [2, T], F32), ("xr", [2, TT, P], F32), ("xk", [2, TT, P], F32), ("fg", [2, P], F32)],
            [("ot_place", [2, T], F32), ("so", [E], F32)],
            [("v", [T], F32), ("u", [T + 2 * CONV_BUF], F32), ("cv", [2, T + CONV_BUF], F32), ("q", [T], F32),
             ("zb_sig", [T], F32), ("zb_silu", [T], F32), ("yrc", [T], F32)])

        raw = tile("raw", [RING, CW])
        hi = tile("hi", [RING, CW], F32R)
        lo = tile("lo", [RING, CW], F32R)
        ident = tile("ident", [P])
        NVEC = KD + 2 * KD + KE + TAPS * KE
        vec = tile("vec", [NVEC])
        HALO = POOL_BUF + CONV_BUF
        state = tile("state", [KE, HALO])
        carry = tile("carry", [KE, HALO])
        zero = tile("zero", [HALO])
        tails = tile("tails", [KE, 2 * HALO])
        ratio = tile("ratio", [NG, POOL_BUF])
        ssq = tile("ssq", [TT])
        var = tile("var", [TT])
        rstd = tile("rstd", [TT])
        ssq1 = tile("ssq1", [TT])
        var1 = tile("var1", [TT])
        rstd1 = tile("rstd1", [TT])
        sums = tile("sums", [KD, TT])
        ssqy = tile("ssqy", [TT])
        vary = tile("vary", [TT])
        rstdy = tile("rstdy", [TT])
        power = tile("power", [TT])
        spill = nc.dram_tensor("spill", (TT * P, D), F32, kind="Internal").ap()

        ps = [ctx.enter_context(nc.psum_tensor(f"ps{b}", [P, 2, 512], F32)) for b in range(4)]
        flat = [b[:, :, :].rearrange("p b n -> p (b n)") for b in ps]
        cols = [b[:, :, 0:HC] for b in ps]

        def two(a):
            return a.rearrange("p (b n) -> p b n", b=2)

        def f32(a):
            return a.bitcast(F32)

        V_G, V_B, V_S, V_W = 0, KD, 3 * KD, 3 * KD + KE

        def per_channel(c):
            return vec[:, bass.ds(c, 1)]

        raw_landed = [sem(f"raw_landed{s}") for s in range(RING)]
        chunk_hi = sem("chunk_hi")
        chunk_lo = sem("chunk_lo")
        chunk_done = sem("chunk_done")
        drained = [sem(f"drained{b}") for b in range(4)]
        const_set = sem("const_set")
        ident_made = sem("ident_made")
        rows_landed = sem("rows_landed")
        setup_transposed = sem("setup_transposed")
        x_landed = [sem(f"x_landed{t}") for t in range(TT)]
        row_squared = sem("row_squared")
        norm_step = sem("norm_step")
        x_scaled = sem("x_scaled")
        h_turned = sem("h_turned")
        states_turned = sem("states_turned")
        turned_back = sem("turned_back")
        side_landed = sem("side_landed")
        side_step = sem("side_step")
        side_stored = sem("side_stored")
        side_done = sem("side_done")
        xk_landed = [sem(f"xk_landed{e}") for e in range(2)]
        xk_scaled = sem("xk_scaled")
        xr_landed = [sem(f"xr_landed{e}") for e in range(2)]
        spilled = [sem(f"spilled{e}") for e in range(2)]
        sum_step = sem("sum_step")
        sum_made = sem("sum_made")
        h_hi = sem("h_hi")
        mix_landed = sem("mix_landed")
        mix_w_hi = sem("mix_w_hi")
        mix_w_lo = sem("mix_w_lo")
        window_step = sem("window_step")
        diff_made = sem("diff_made")
        diff_hi = sem("diff_hi")
        diff_split = sem("diff_split")
        za_sigmoid = sem("za_sigmoid")
        mix_done = sem("mix_done")
        conv_step = sem("conv_step")
        zb_sigmoid = sem("zb_sigmoid")
        y_raw = sem("y_raw")
        y_hi = sem("y_hi")
        y_split = sem("y_split")
        merged = sem("merged")
        merged_hi = sem("merged_hi")
        merged_split = sem("merged_split")
        res_landed = sem("res_landed")
        first_columns_made = sem("first_columns_made")
        first_columns_out = sem("first_columns_out")
        first_tiles_turned = sem("first_tiles_turned")
        first_tiles_summed = sem("first_tiles_summed")
        first_tiles_norm = sem("first_tiles_norm")
        first_tiles_made = sem("first_tiles_made")
        y_normed_dve = sem("y_normed_dve")
        y_normed_act = sem("y_normed_act")
        y_stored = sem("y_stored")
        states_stored = sem("states_stored")

        win_v = w_in[0].rearrange("(kh kt p) (b c) -> kh b p kt c", kh=2, p=P, c=P)
        wout_v = w_out[0].rearrange("(kh kt p) (b c) -> kh b p kt c", kh=2, p=P, c=P)
        wpp_v = w_proj_pool[0].rearrange("(kt p) (b c) -> b p kt c", p=P, c=P)
        wpc_v = w_proj_conv[0].rearrange("(kt p) (b c) -> b p kt c", p=P, c=P)
        mix_v = w_pool_mix[0].rearrange("g (kt p) d -> g p kt d", p=P)

        def token_runs(half, prompt, sample):
            out = []
            for first, n in SEGS[half]:
                t = first
                while t < first + n:
                    k = min(P - t % P, first + n - t)
                    if half == 1 and t >= CUT:
                        rows = sample[0, t - CUT:t - CUT + k, :]
                    else:
                        rows = prompt[0, half * T + t:half * T + t + k, :]
                    out.append((t // P, t % P, rows))
                    t += k
            return out

        def x_blocks(half, kt, dst):
            out = []
            for t0, n, src in ((0, T, x_prompt[0, 0:T]),) if half == 0 else \
                    ((0, CUT, x_prompt[0, T:SEQ]), (CUT, T - CUT, x_sample[0])):
                t = 0
                while t < n:
                    tt, p0 = divmod(t0 + t, P)
                    whole = (n - t) // P if p0 == 0 else 0
                    if whole:
                        k = whole * P
                        cols_ = None if dst is None else (
                            dst[:, tt:tt + whole, :],
                            src[t:t + k, bass.ds(kt * P, P)].rearrange("(t p) c -> p t c", p=P))
                    else:
                        k = min(P - p0, n - t)
                        cols_ = None if dst is None else (dst[p0:p0 + k, tt, :], src[t:t + k, bass.ds(kt * P, P)])
                    out.append(cols_)
                    t += k
            return out

        def spill_blocks(e, src):
            full_ = (TT - 1) * P
            return [(spill[0:full_, bass.ds(e * P, P)].rearrange("(t p) c -> p t c", p=P), src[:, 0:TT - 1, :]),
                    (spill[full_:T, bass.ds(e * P, P)], src[0:TL, TT - 1, :])]

        X_RUNS = [token_runs(hf, x_prompt, x_sample) for hf in range(HALVES)]
        Y_RUNS = [token_runs(hf, y_prompt, y_sample) for hf in range(HALVES)]
        XK_DMAS = len(x_blocks(1, 0, None))
        XR_DMAS = len(x_blocks(0, 0, None)) + 1

        ACT_TILES = list(range(FT + 1, TT - 1))
        DVE_TILES = [tt for tt in range(TT) if tt not in ACT_TILES]
        SHORT_FIRST = [TT - 1, *range(TT - 1)]

        def rows_of(tt):
            return P if tt < TT - 1 else TL

        def spans(eng, half, phase, peel_first=False, peel_last=False):
            n = PHASES[phase][0]
            a, b = int(peel_first), n - int(peel_last)
            if peel_first:
                yield 0
            with eng.Fori(a, b) as i:
                yield i
            if peel_last:
                yield n - 1

        def settled(eng, half, phase):
            for b in range(4):
                eng.wait_ge(drained[b], base[f"drained{b}", half, phase])

        block = ctx.enter_context(nc.Block())

        @block.sync
        def _(sp):
            def load(n, k, src, wait=True):
                if wait:
                    sp.wait_ge(chunk_lo, n - RING + 1)
                sp.dma_start(raw[:, k % RING, :].rearrange("p (kt c) -> p kt c", c=P), src) \
                    .then_inc(raw_landed[k % RING], 16)

            for r, src in ((V_G, norm_g[0].rearrange("(r c) -> r c", c=P)),
                           (V_B, b_gate[0].rearrange("(r c) -> r c", c=P)),
                           (V_S, pool_scale[0].rearrange("(r c) -> r c", c=P)),
                           (V_W, w_conv[0].rearrange("w (r c) -> (w r) c", c=P))):
                sp.dma_start(vec_rows[r:r + src.shape[0], :], src).then_inc(rows_landed, 16)
            sp.dma_start(state_rows[0:POOL_BUF, :], state_pool[0, 0]).then_inc(rows_landed, 16)
            sp.dma_start(state_rows[POOL_BUF:HALO, :], state_conv[0, 0]).then_inc(rows_landed, 16)

            sp.wait_ge(x_landed[SHORT_FIRST[-2]], 16)

            for half in range(HALVES):
                for i in spans(sp, half, "pool", peel_first=half == 0):
                    c0 = at("chunk", half, "pool", i, 0)
                    for k in range(8):
                        blk = (B_XA, B_ZA)[k // 4] + (k // 2) % 2
                        load(c0 + k, k, win_v[k % 2, 2 * i + blk], wait=not (isinstance(i, int) and k < RING))
                        if k == 3:
                            if half == 1:
                                sp.wait_ge(chunk_done, base["chunk", half, "pool"])
                            if not isinstance(i, int):
                                sp.wait_ge(mix_w_lo, at("mix_w_lo", half, "pool", i, 0))
                            sp.dma_start(mix_raw[:, :].rearrange("p (kt d) -> p kt d", d=GROUP), mix_v[i]) \
                                .then_inc(mix_landed, 16)
                for i in spans(sp, half, "mergeA"):
                    c0 = at("chunk", half, "mergeA", i, 0)
                    for k, (ii, r) in enumerate(ROLES):
                        load(c0 + k, k, wpp_v[MU * i + ii] if r == 2 else win_v[r, B_GA + MU * i + ii])
                for i in spans(sp, half, "conv"):
                    c0 = at("chunk", half, "conv", i, 0)
                    for k in range(8):
                        load(c0 + k, k, win_v[k % 2, (B_V, B_CG, B_BG, B_ZB)[k // 2] + i])
                for i in spans(sp, half, "mergeB"):
                    c0 = at("chunk", half, "mergeB", i, 0)
                    for k, (ii, r) in enumerate(ROLES):
                        load(c0 + k, k, wpc_v[MU * i + ii] if r == 2 else win_v[r, B_GB + MU * i + ii])
                out = f"out{half}"
                for i in spans(sp, half, out):
                    c0 = at("chunk", half, out, i, 0)
                    for k in range(4):
                        load(c0 + k, k, wout_v[k % 2, 2 * i + k // 2])
            for tt, p0, rows in Y_RUNS[1]:
                if tt in DVE_TILES:
                    sp.wait_ge(y_normed_dve, DVE_TILES.index(tt) + 1)
                    sp.dma_start(rows, res[p0:p0 + rows.shape[0], tt, :]).then_inc(y_stored, 16)
            sp.wait_ge(y_stored, 16 * len(Y_RUNS[1]))

        @block.gpsimd
        def _(pool):
            nc.gpsimd.memset(ident[:, :], 0.0).then_inc(ident_made, 1)
            pool.wait_ge(ident_made, 1)
            nc.gpsimd.affine_select(out=ident[:, :], in_=ident[:, :], compare_op=ALU.not_equal, fill=1.0,
                                    base=0, pattern=[[-1, P]], channel_multiplier=1).then_inc(ident_made, 1)
            nc.gpsimd.memset(zero[:, :], 0.0).then_inc(const_set, 1)
            nc.gpsimd.memset(ratio[:, :, :], 1.0).then_inc(const_set, 1)
            pool.wait_ge(const_set, 2)
            for g, w in enumerate(WINDOWS):
                for t in range(w - 1):
                    last = nc.gpsimd.memset(ratio[:, g, t:t + 1], w / (t + 1))
            last.then_inc(const_set, 1)
            nc.gpsimd.memset(power[:, :], -0.5).then_inc(const_set, 1)
            nc.gpsimd.memset(sums[:, :, :], 1.0).then_inc(const_set, 1)
            nc.gpsimd.memset(ssq1[:, :], 1.0).then_inc(const_set, 1)
            pool.wait_ge(const_set, 6)

            def raise_(dst, src, r, c, value):
                pool.wait_ge(norm_step, value)
                nc.gpsimd.tensor_tensor(dst[0:r, c], src[0:r, c], power[0:r, c], ALU.pow).then_inc(norm_step, 1)

            for n, tt in enumerate(SHORT_FIRST):
                raise_(rstd, var, rows_of(tt), slice(tt, tt + 1), at("norm_step", 0, "norm", n, 1))

            steps, landed = 0, 0
            pool.wait_ge(x_scaled, TT + 1)
            for tt in range(TT):
                r = rows_of(tt)
                if tt > 0:
                    pool.wait_ge(side_step, steps)
                for t, p0, rows in X_RUNS[1]:
                    if t == tt:
                        landed += 16
                        pool.dma_start(side[p0:p0 + rows.shape[0], :], rows).then_inc(side_landed, 16)
                pool.wait_ge(side_landed, landed)
                nc.gpsimd.tensor_tensor(side[0:r, :], side[0:r, :], side[0:r, :], ALU.mult).then_inc(side_step, 1)
                pool.wait_ge(side_step, steps + 1)
                n = D // 2
                k = 1
                while n >= 1:
                    dst = side[0:r, 0:n] if n > 1 else ssq1[0:r, tt:tt + 1]
                    nc.gpsimd.tensor_tensor(dst, side[0:r, 0:n], side[0:r, n:2 * n], ALU.add).then_inc(side_step, 1)
                    k += 1
                    pool.wait_ge(side_step, steps + k)
                    n //= 2
                steps += k
            nc.gpsimd.tensor_scalar(var1[:, :], ssq1[:, :], 1.0 / D, EPS, ALU.mult, ALU.add).then_inc(side_step, 1)
            pool.wait_ge(side_step, steps + 1)
            nc.gpsimd.tensor_tensor(rstd1[:, :], var1[:, :], power[:, :], ALU.pow).then_inc(side_done, 1)

            def load_x(i, e):
                for dst, src in x_blocks(0, 2 * i + e, xr[:, e]):
                    pool.dma_start(dst, src).then_inc(xr_landed[e], 16)
                pool.dma_start(fg[:, e, :], final_norm_g[bass.ds((2 * i + e) * P, P)].rearrange("(a d) -> a d", a=1)
                               .broadcast_to([P, P])).then_inc(xr_landed[e], 16)

            settled(pool, 0, "out0")
            pool.wait_ge(merged, at("merged", 0, "mergeB", PHASES["mergeB"][0], 0))
            for e in range(2):
                load_x(0, e)
            for i in spans(pool, 0, "out0", peel_last=True):
                for e in range(2):
                    pool.wait_ge(sum_made, at("sum_made", 0, "out0", i, e + 1))
                    for dst, src in spill_blocks(2 * i + e, xr[:, e]):
                        pool.dma_start(dst, src).then_inc(spilled[e], 16)
                    if not isinstance(i, int):
                        pool.wait_ge(spilled[e], 32 * i + 32)
                        load_x(i + 1, e)

            raise_(rstdy, vary, P, slice(0, TT), at("norm_step", 0, "final", 0, 2))
            pool.wait_ge(norm_step, at("norm_step", 0, "final", 0, 3))
            for e in range(2):
                pool.wait_ge(spilled[e], 32 * (KD // 2))
            settled(pool, 1, "pool")
            kept, steps = 0, steps + 1
            for tt in range(TT):
                r = rows_of(tt)
                if tt > 0:
                    pool.wait_ge(side_stored, 16 * kept)
                landed += 16
                pool.dma_start(side[0:r, :], spill[tt * P:tt * P + r, :]).then_inc(side_landed, 16)
                pool.wait_ge(side_landed, landed)
                steps += 1
                nc.gpsimd.tensor_scalar(side[0:r, :], side[0:r, :], rstdy[0:r, tt:tt + 1], None, ALU.mult) \
                    .then_inc(side_step, 1)
                pool.wait_ge(side_step, steps)
                for t, p0, rows in Y_RUNS[0]:
                    if t == tt:
                        kept += 1
                        pool.dma_start(rows, side[p0:p0 + rows.shape[0], :]).then_inc(side_stored, 16)
            pool.wait_ge(side_stored, 16 * kept)
            nc.gpsimd.memset(ssq1[:, :], 1.0).then_inc(side_done, 1)

            pool.wait_ge(first_tiles_norm, 2)
            nc.gpsimd.tensor_tensor(rstdy[:, 0:FT], vary[:, 0:FT], power[:, 0:FT], ALU.pow) \
                .then_inc(first_tiles_norm, 1)
            raise_(rstdy, vary, P, slice(FT, TT), at("norm_step", 1, "final", 0, 2))

        @block.tensor
        def _(pe):
            def buffer(b, half, phase, i, use):
                pe.wait_ge(drained[b], at(f"drained{b}", half, phase, i, use))

            def product(b, n, k, rhs, start, stop, each=None, kt0=0, banks=range(2), signal=chunk_done):
                pe.wait_ge(chunk_lo, n + 1)
                s = k % RING
                for kt in range(CK):
                    if each is not None:
                        each(kt0 + kt)
                    for w, part in ((hi, 0), (hi, 1), (lo, 0)):
                        for c in banks:
                            first = start and kt == 0 and w is hi and part == 0
                            last = stop and kt == CK - 1 and w is lo
                            mm = nc.tensor.matmul(ps[b][:, c, 0:HC], w[:, s, kt * P:(kt + 1) * P],
                                                  rhs(kt, part)[:, c * HC:(c + 1) * HC], start=first, stop=last)
                if signal is not None:
                    mm.then_inc(signal, 1)

            def full(b, half, phase, i, k, src, each=None):
                n = at("chunk", half, phase, i, k)
                for kh in range(2):
                    product(b, n + kh, k + kh, lambda kt, part: src[:, CK * kh + kt, part, :], kh == 0, kh == 1,
                            each, CK * kh)

            pe.wait_ge(ident_made, 2)

            def turn(b, src):
                for tt in range(TT):
                    r = rows_of(tt)
                    last = nc.tensor.transpose(flat[b][:, tt * P:tt * P + r], src(tt, r), ident[0:r, 0:r])
                last.then_inc(h_turned, 1)

            def first_turn(kt):
                b = 1 + kt % TURNS
                pe.wait_ge(drained[b], base[f"drained{b}", 0, "prep"] + kt // TURNS)
                turn(b, lambda tt, r: xn[0:r, tt, kt * P:(kt + 1) * P])

            def first_h(kt):
                b = 1 + kt % TURNS
                pe.wait_ge(drained[b], base[f"drained{b}", 0, "prep"] + kt // TURNS + 1)
                if kt + TURNS < KD:
                    first_turn(kt + TURNS)

            for n, tt in enumerate(SHORT_FIRST):
                if n == TT - 2:
                    pe.wait_ge(rows_landed, 96)
                    nc.tensor.transpose(flat[0][:, 0:NVEC], vec_rows[0:NVEC, :], ident[0:NVEC, 0:NVEC]) \
                        .then_inc(setup_transposed, 1)
                    for j in range(KE):
                        last = nc.tensor.transpose(flat[0][:, 512 + 32 * j:512 + 32 * j + HALO],
                                                   state_rows[0:HALO, j * P:(j + 1) * P],
                                                   ident[0:HALO, 0:HALO])
                    last.then_inc(setup_transposed, 1)
                pe.wait_ge(x_scaled, n + 1)
                for kt in range(TURNS):
                    r = rows_of(tt)
                    last = nc.tensor.transpose(flat[1 + kt][:, tt * P:tt * P + r], xn[0:r, tt, kt * P:(kt + 1) * P],
                                               ident[0:r, 0:r])
                    if n == TT - 1:
                        last.then_inc(h_turned, 1)
            pe.wait_ge(x_scaled, TT + 1)

            def back(half, i, e, use, tiles=range(TT), signal=turned_back):
                out = f"out{half}"
                if signal is first_tiles_turned:
                    pe.wait_ge(first_columns_out, 1)
                else:
                    pe.wait_ge(drained[e], at(f"drained{e}", half, out, i, 1))
                buffer(2 + e, half, out, i, use)
                for tt in tiles:
                    r = rows_of(tt)
                    last = nc.tensor.transpose(flat[2 + e][0:r, tt * P:(tt + 1) * P],
                                               ot[:, e, tt * P:tt * P + r], ident[:, :])
                last.then_inc(signal, 1)

            def second_h(kt):
                if kt == CK:
                    back(0, PHASES["out0"][0] - 1, 1, 1)
                if kt >= KD - 2:
                    b = 2 + kt - (KD - 2)
                    pe.wait_ge(drained[b], base[f"drained{b}", 1, "pool"] - 1)

            for half in range(HALVES):
                for i in spans(pe, half, "pool", peel_first=True):
                    for k, b, use in ((0, 0, 0), (2, 1, 0), (4, 2, 0), (6, 0, 1)):
                        first = isinstance(i, int) and k == 0
                        buffer(b, half, "pool", i, use)
                        full(b, half, "pool", i, k, h, (first_h, second_h)[half] if first else None)
                    pe.wait_ge(mix_w_lo, at("mix_w_lo", half, "pool", i, 1))
                    pe.wait_ge(diff_split, at("diff_split", half, "pool", i, 2))
                    for j, b, use in ((0, 1, 1), (1, 3, 0)):
                        buffer(b, half, "pool", i, use)
                        for kt in range(GJ):
                            for w, part in ((mix_hi, 0), (mix_hi, 1), (mix_lo, 0)):
                                for c in range(2):
                                    mm = nc.tensor.matmul(
                                        ps[b][:, c, 0:HC], w[:, kt * GROUP + j * P:kt * GROUP + (j + 1) * P],
                                        ds[:, kt, part, c * HC:(c + 1) * HC],
                                        start=kt == 0 and w is mix_hi and part == 0,
                                        stop=kt == GJ - 1 and w is mix_lo)
                        mm.then_inc(mix_done, 1)

                def merge(phase):
                    def branch(i, ii, k):
                        b = 2 * (ii % 2)
                        if ii == 0:
                            last_y = {"mergeA": ("pool", NG), "mergeB": ("conv", KE)}[phase]
                            pe.wait_ge(y_split, at("y_split", half, *last_y, 0))
                        buffer(b, half, phase, i, ii // 2)
                        product(b, at("chunk", half, phase, i, k), k, lambda kt, part: y[:, kt, part, :],
                                True, True)

                    for i in spans(pe, half, phase):
                        for k, (ii, r) in enumerate(ROLES):
                            if r == 2:
                                branch(i, ii, k)
                            if r == 0:
                                b = 2 * (ii % 2) + 1
                                buffer(b, half, phase, i, ii // 2)
                                full(b, half, phase, i, k, h)

                merge("mergeA")
                for i in spans(pe, half, "conv"):
                    for b in range(4):
                        buffer(b, half, "conv", i, 0)
                        full(b, half, "conv", i, 2 * b, h)
                merge("mergeB")

                out = f"out{half}"

                def next_h(i, e):
                    if half == 0:
                        pe.wait_ge(xk_scaled, at("xk_scaled", 0, out, i, e + 1))
                        buffer(2 + e, 0, out, i, 0)
                        turn(2 + e, lambda tt, r: xk[0:r, e, tt, :])

                def new_states():
                    pe.wait_ge(zb_sigmoid, at("zb_sigmoid", half, "conv", KE, 0))
                    buffer(3, half, "state", 0, 0)
                    for j in range(KE):
                        last = nc.tensor.transpose(flat[3][0:2 * HALO, j * P:(j + 1) * P], tails[:, j, :],
                                                   ident[:, :])
                    last.then_inc(states_turned, 1)

                def last_block(i):
                    def first_back(kt):
                        if kt == 2:
                            back(half, i, 1, 0, range(FT), first_tiles_turned)

                    buffer(1, half, out, i, 0)
                    for c in range(2):
                        for k in (2, 3):
                            product(1, at("chunk", half, out, i, k), k,
                                    lambda kt, part: ms[:, CK * (k % 2) + kt, part, :], k == 2, k == 3,
                                    first_back if (c, k) == (1, 2) else None, 0, [c],
                                    chunk_done if c == 1 else first_columns_made if k == 3 else None)
                            if (c, k) == (0, 2):
                                back(half, i, 0, 0)
                    pe.wait_ge(first_tiles_summed, 1)
                    back(half, i, 1, 0, range(FT, TT))

                turned_use = 1 if half == 0 else 0
                for i in spans(pe, half, out, peel_first=True, peel_last=half == 1):
                    first = isinstance(i, int) and i == 0
                    each = None
                    if first:
                        each = lambda kt: pe.wait_ge(merged_split, at("merged_split", half, "split", kt, 1))
                    for k in range(4):
                        if isinstance(i, int) and not first and k == 2:
                            last_block(i)
                            break
                        if k % 2 == 0:
                            buffer(k // 2, half, out, i, 0)
                        product(k // 2, at("chunk", half, out, i, k), k,
                                lambda kt, part: ms[:, CK * (k % 2) + kt, part, :], k % 2 == 0, k % 2 == 1,
                                each if k < 2 else None, CK * (k % 2))
                        if k == 0 and not first:
                            back(half, i - 1, 1, turned_use)
                        if k == 0 and first and half == 1:
                            new_states()
                        if k == 2:
                            back(half, i, 0, turned_use)
                        if k % 2 == 1:
                            next_h(i, k // 2)

        @block.scalar
        def _(act):
            def ahead(half, phase, i, k):
                n = at("chunk", half, phase, i, k)
                act.wait_ge(chunk_done, n + 1)
                s = k % RING
                act.wait_ge(raw_landed[s], (16 // RING) * (n - s) + 32)
                nc.scalar.activation(hi[:, s, :], raw[:, s, :], ACT.Copy).then_inc(chunk_hi, 1)

            def done(half, phase, i, k):
                act.wait_ge(chunk_done, at("chunk", half, phase, i, k) + 1)

            def first_split(s):
                act.wait_ge(raw_landed[s], 16)
                nc.scalar.activation(hi[:, s, :], raw[:, s, :], ACT.Copy).then_inc(chunk_hi, 1)

            for tt, p0, rows in X_RUNS[0][-1:] + X_RUNS[0][:-1]:
                act.dma_start(xn[p0:p0 + rows.shape[0], tt, :], rows).then_inc(x_landed[tt], 16)
            for n, tt in enumerate(SHORT_FIRST):
                r = rows_of(tt)
                act.wait_ge(x_landed[tt], 16)
                if n > 0:
                    act.wait_ge(row_squared, n)
                nc.scalar.activation(junk[0:r, :], xn[0:r, tt, :], ACT.Square,
                                     accum_out=ssq[0:r, tt:tt + 1]).then_inc(row_squared, 1)
            act.wait_ge(const_set, 6)
            act.wait_ge(drained[0], 2)
            for kt in range(KD):
                if kt % 4 == 0:
                    first_split(kt // 4)
                b = 1 + kt % TURNS
                act.wait_ge(h_turned, kt + 1)
                nc.scalar.activation(h[:, kt, 0, :], flat[b][:, 0:T], ACT.Copy,
                                     scale=per_channel(V_G + kt)).then_inc(h_hi, 1)

            for half in range(HALVES):
                settled(act, half, "pool")
                for i in spans(act, half, "pool"):
                    for k in range(8):
                        if k in (5, 7):
                            j = (k - 5) // 2
                            done(half, "pool", i, k)
                            nc.scalar.activation(two(za_sig[:, j, :]), cols[(2, 0)[j]], ACT.Sigmoid) \
                                .then_inc(za_sigmoid, 1)
                        ahead(half, "pool", i, k)
                        if k == 4:
                            act.wait_ge(mix_landed, at("mix_landed", half, "pool", i, 16))
                            nc.scalar.activation(mix_hi[:, :], mix_raw[:, :], ACT.Copy).then_inc(mix_w_hi, 1)
                        if k in (1, 3):
                            j = k // 2
                            act.wait_ge(diff_made, at("diff_made", half, "pool", i, j + 1 - 2))
                            jb = 2 * i + j
                            left = zero[:, 0:POOL_BUF] if half == 0 else carry[:, jb, 0:POOL_BUF]
                            nc.scalar.copy(xe[:, j, 0:POOL_BUF], left)
                            if half == 1:
                                c = ext(1, CUT, POOL_BUF) - POOL_BUF
                                nc.scalar.copy(xe[:, j, c:c + POOL_BUF], state[:, jb, 0:POOL_BUF])
                            for s, (first, n) in enumerate(SEGS[half]):
                                c = first + n - POOL_BUF - HC
                                dst = carry[:, jb, 0:POOL_BUF] if half == 0 else \
                                    tails[:, jb, s * POOL_BUF:(s + 1) * POOL_BUF]
                                nc.scalar.copy(dst, ps[j][:, 1, c:c + POOL_BUF])
                            for bank, c, first, n in PIECES[half]:
                                e0 = ext(half, first, POOL_BUF)
                                last = nc.scalar.copy(xe[:, j, e0:e0 + n], ps[j][:, bank, c:c + n])
                            last.then_inc(drained[j], 1)
                        if k in (2, 4):
                            j = k // 2 - 1
                            act.wait_ge(diff_made, at("diff_made", half, "pool", i, j + 1))
                            nc.scalar.copy(ds[:, j, 0, :], dr[:, j, :]).then_inc(diff_hi, 1)
                    for j, b, use in ((0, 1, 2), (1, 3, 1)):
                        act.wait_ge(drained[b], at(f"drained{b}", half, "pool", i, use))
                        nc.scalar.copy(y[:, 2 * i + j, 0, :], yrp[:, j, :]).then_inc(y_hi, 1)

                def merged_split_hi(s):
                    if 2 * s >= KD:
                        act.wait_ge(merged_split, at("merged_split", half, "split", 2 * s - KD, 1))
                    nc.scalar.copy(ms[:, s, 0, :], m[:, s, :]).then_inc(merged_hi, 1)

                def merge(phase, bias0, peel_last=False):
                    settled(act, half, phase)
                    for i in spans(act, half, phase, peel_last=peel_last):
                        for k in range(3 * MU):
                            ahead(half, phase, i, k)
                            if peel_last and isinstance(i, int) and k in (3 * MU - 3, 3 * MU - 2):
                                act.wait_ge(merged, at("merged", half, phase, i, MU - 1))
                                n = EARLY // 2
                                s0 = 0 if k == 3 * MU - 3 else n
                                for s in range(s0, s0 + n):
                                    merged_split_hi(s)
                            if k % 3 == 2:
                                ii = k // 3
                                g = ii % 2
                                nc.scalar.activation(two(gate[:, g, :]), cols[2 * g + 1], ACT.Sigmoid,
                                                     bias=per_channel(bias0 + MU * i + ii)) \
                                    .then_inc(drained[2 * g + 1], 1)

                merge("mergeA", V_B)

                settled(act, half, "conv")
                act.wait_ge(side_done, half + 1)
                for i in spans(act, half, "conv"):
                    for k in range(8):
                        ahead(half, "conv", i, k)
                        if k == 1:
                            left = zero[:, 0:CONV_BUF] if half == 0 else carry[:, i, POOL_BUF:HALO]
                            nc.scalar.copy(u[:, 0:CONV_BUF], left)
                            if half == 1:
                                c = ext(1, CUT, CONV_BUF) - CONV_BUF
                                nc.scalar.copy(u[:, c:c + CONV_BUF], state[:, i, POOL_BUF:HALO])
                            nc.scalar.copy(two(v[:, :]), cols[0]).then_inc(drained[0], 1)
                        if k == 4:
                            act.wait_ge(drained[1], at("drained1", half, "conv", i, 1))
                            for s, (first, n) in enumerate(SEGS[half]):
                                c = ext(half, first + n - 1, CONV_BUF) + 1 - CONV_BUF
                                d0 = 2 * POOL_BUF + s * CONV_BUF
                                dst = carry[:, i, POOL_BUF:HALO] if half == 0 else tails[:, i, d0:d0 + CONV_BUF]
                                nc.scalar.copy(dst, u[:, c:c + CONV_BUF])
                        if k == 7:
                            nc.scalar.activation(two(zb_sig[:, :]), cols[3], ACT.Sigmoid).then_inc(zb_sigmoid, 1)
                    act.wait_ge(y_raw, at("y_raw", half, "conv", i, 1))
                    nc.scalar.copy(y[:, i, 0, :], yrc[:, :]).then_inc(y_hi, 1)

                def load_xk(i, e):
                    for dst, src in x_blocks(1, 2 * i + e, xk[:, e]):
                        act.dma_start(dst, src).then_inc(xk_landed[e], 16)

                if half == 0:
                    act.wait_ge(y_split, at("y_split", half, "conv", KE, 0))
                    settled(act, half, "mergeB")
                    for e in range(2):
                        load_xk(0, e)
                merge("mergeB", V_B + KD, peel_last=True)
                act.wait_ge(merged, at("merged", half, "mergeB", PHASES["mergeB"][0], 0))
                for s in range(EARLY, KD):
                    merged_split_hi(s)

                out = f"out{half}"
                for b in range(4):
                    act.wait_ge(drained[b], base[f"drained{b}", half, "state" if (half, b) == (1, 3) else out])
                if half == 1:
                    for tt, p0, rows in X_RUNS[1]:
                        act.dma_start(res[p0:p0 + rows.shape[0], tt, :], rows).then_inc(res_landed, 16)
                    act.dma_start(fin_g[:, :], final_norm_g.rearrange("(a d) -> a d", a=1)
                                  .broadcast_to([P, D])).then_inc(res_landed, 16)

                def store_states():
                    act.wait_ge(drained[3], at("drained3", half, "state", 0, 1))
                    r = 0
                    for dst in (new_pool_prompt, new_pool_sample, new_conv_prompt, new_conv_sample):
                        n = dst.shape[2]
                        act.dma_start(dst[0, 0], so[r:r + n, :]).then_inc(states_stored, 16)
                        r += n

                def next_h_hi(i, e):
                    act.wait_ge(h_turned, at("h_turned", 0, out, i, e + 1))
                    nc.scalar.activation(h[:, 2 * i + e, 0, :], flat[2 + e][:, 0:T], ACT.Copy,
                                         scale=per_channel(V_G + 2 * i + e)).then_inc(h_hi, 1)

                for i in spans(act, half, out, peel_last=True):
                    for k in range(4):
                        e = k // 2
                        if half == 1 and isinstance(i, int) and k == 2:
                            act.wait_ge(first_columns_made, 1)
                            nc.scalar.copy(ot[:, e, 0:HC], ps[e][:, 0, 0:HC]).then_inc(first_columns_out, 1)
                            continue
                        done(half, out, i, k)
                        if half == 1 and isinstance(i, int) and k == 3:
                            nc.scalar.copy(ot[:, e, HC:T], ps[e][:, 1, 0:HC]).then_inc(drained[e], 1)
                        elif k % 2 == 1:
                            nc.scalar.copy(two(ot[:, e, :]), cols[e]).then_inc(drained[e], 1)
                        if not (half == 1 and isinstance(i, int)):
                            ahead(half, out, i, k)
                        if half == 1 and isinstance(i, int) and k == 0:
                            store_states()
                        if k % 2 == 1:
                            if half == 0:
                                next_h_hi(i, e)
                                if not isinstance(i, int):
                                    load_xk(i + 1, e)

            act.wait_ge(norm_step, at("norm_step", 1, "final", 0, 3))
            act.wait_ge(sum_made, at("sum_made", 1, "out1", PHASES["out1"][0], 0))
            n = 0
            for tt in ACT_TILES:
                nc.scalar.activation(res[:, tt, :], res[:, tt, :], ACT.Copy, scale=rstdy[:, tt:tt + 1]) \
                    .then_inc(y_normed_act, 1)
                n += 1
                act.wait_ge(y_normed_act, n)
                for t, p0, rows in Y_RUNS[1]:
                    if t == tt:
                        act.dma_start(rows, res[p0:p0 + rows.shape[0], tt, :]).then_inc(y_stored, 16)
            act.wait_ge(states_stored, 64)
            act.wait_ge(y_stored, 16 * len(Y_RUNS[1]))

        @block.vector
        def _(dve):
            def split(n, s):
                dve.wait_ge(chunk_hi, n + 1)
                nc.vector.tensor_tensor(lo[:, s, :], raw[:, s, :], f32(hi[:, s, :]), ALU.subtract) \
                    .then_inc(chunk_lo, 1)

            def ahead(half, phase, i, k):
                split(at("chunk", half, phase, i, k) + RING, k % RING)

            def y_lo(half, phase, i, k, jb, src):
                dve.wait_ge(y_hi, at("y_hi", half, phase, i, k))
                nc.vector.tensor_tensor(y[:, jb, 1, :], src, f32(y[:, jb, 0, :]), ALU.subtract) \
                    .then_inc(y_split, 1)

            steps = [0]

            def window_link(ins):
                steps[0] += 1
                ins.then_inc(window_step, 1)
                dve.wait_ge(window_step, steps[0])

            nc.vector.memset(var[:, :], 0.0).then_inc(diff_made, 2)
            dve.wait_ge(const_set, 6)
            dve.wait_ge(diff_made, 2)

            for n, tt in enumerate(SHORT_FIRST):
                r = rows_of(tt)
                if n == TT - 1:
                    dve.wait_ge(setup_transposed, 1)
                    nc.vector.tensor_copy(vec[:, :], flat[0][:, 0:NVEC]).then_inc(drained[0], 1)
                    dve.wait_ge(setup_transposed, 2)
                    nc.vector.tensor_copy(state[:, :, :], flat[0][:, 512:512 + 32 * KE].rearrange(
                        "p (j n) -> p j n", n=32)[:, :, 0:HALO]).then_inc(drained[0], 1)
                    dve.wait_ge(drained[0], 2)
                dve.wait_ge(row_squared, n + 1)
                nc.vector.tensor_scalar(var[0:r, tt:tt + 1], ssq[0:r, tt:tt + 1], 1.0 / D, EPS, ALU.mult, ALU.add) \
                    .then_inc(norm_step, 1)
                dve.wait_ge(norm_step, at("norm_step", 0, "norm", n, 2))
                for c in [slice(0, D)] if n < TT - 1 else [slice(0, TURNS * P), slice(TURNS * P, D)]:
                    nc.vector.tensor_scalar(xn[0:r, tt, c], xn[0:r, tt, c], rstd[0:r, tt:tt + 1], None, ALU.mult) \
                        .then_inc(x_scaled, 1)

            def h_lo(kt, b, value):
                dve.wait_ge(h_hi, value)
                nc.vector.scalar_tensor_tensor(h[:, kt, 1, :], flat[b][:, 0:T], per_channel(V_G + kt),
                                               f32(h[:, kt, 0, :]), ALU.mult, ALU.subtract) \
                    .then_inc(drained[b], 1)

            for kt in range(KD):
                if kt % 4 == 0:
                    split(kt // 4, kt // 4)
                h_lo(kt, 1 + kt % TURNS, kt + 1)

            for half in range(HALVES):
                for g, w in enumerate(WINDOWS):
                    def mixed_out(j, b, za, use):
                        dve.wait_ge(mix_done, at("mix_done", half, "pool", g, j + 1))
                        dve.wait_ge(drained[za], at(f"drained{za}", half, "pool", g, use))
                        nc.vector.scalar_tensor_tensor(two(yrp[:, j, :]), cols[b], per_channel(V_S + 2 * g + j),
                                                       two(za_silu[:, j, :]), ALU.mult, ALU.mult) \
                            .then_inc(drained[b], 1)

                    for k in range(8):
                        if k in (5, 7):
                            j = (k - 5) // 2
                            dve.wait_ge(za_sigmoid, at("za_sigmoid", half, "pool", g, j + 1))
                            b = (2, 0)[j]
                            if half == 1 and g == 0 and j == 0:
                                for e in range(2):
                                    dve.wait_ge(spilled[e], 32 * (KD // 2))
                            nc.vector.tensor_tensor(two(za_silu[:, j, :]), cols[b], two(za_sig[:, j, :]),
                                                    ALU.mult).then_inc(drained[b], 1)
                        if k == 7:
                            mixed_out(0, 1, 2, 1)
                        ahead(half, "pool", g, k)
                        if k == 4:
                            dve.wait_ge(mix_w_hi, at("mix_w_hi", half, "pool", g, 1))
                            nc.vector.tensor_tensor(mix_lo[:, :], mix_raw[:, :], f32(mix_hi[:, :]), ALU.subtract) \
                                .then_inc(mix_w_lo, 1)
                        if k in (1, 3):
                            j = k // 2
                            width = ext(half, T - 1, POOL_BUF) + 1
                            dve.wait_ge(drained[j], at(f"drained{j}", half, "pool", g, 1))
                            src, reach, n = xe[:, j, :], 0, 1
                            while n < w:
                                dst = ws[:, n.bit_length() % 2, :]
                                lo_c = reach + n
                                window_link(nc.vector.tensor_tensor(
                                    dst[:, lo_c:width], src[:, lo_c:width], src[:, lo_c - n:width - n], ALU.add))
                                src, reach, n = dst, lo_c, 2 * n
                            if half == 0:
                                s0 = src[:, POOL_BUF:2 * POOL_BUF]
                                window_link(nc.vector.tensor_tensor(s0, s0, ratio[:, g, :], ALU.mult))
                            for first, n in SEGS[half]:
                                e0 = ext(half, first, POOL_BUF)
                                last = nc.vector.scalar_tensor_tensor(
                                    dr[:, j, first:first + n], src[:, e0:e0 + n], 1.0 / w, xe[:, j, e0:e0 + n],
                                    ALU.mult, ALU.subtract)
                            last.then_inc(diff_made, 1)
                        if k in (2, 4):
                            j = k // 2 - 1
                            dve.wait_ge(diff_hi, at("diff_hi", half, "pool", g, j + 1))
                            nc.vector.tensor_tensor(ds[:, j, 1, :], dr[:, j, :], f32(ds[:, j, 0, :]), ALU.subtract) \
                                .then_inc(diff_split, 1)
                    mixed_out(1, 3, 0, 2)
                    for j in range(GJ):
                        y_lo(half, "pool", g, j + 1, 2 * g + j, yrp[:, j, :])

                for i in spans(dve, half, "mergeA"):
                    for k in range(3 * MU):
                        ahead(half, "mergeA", i, k)
                        if k % 3 == 2:
                            ii = k // 3
                            b = 2 * (ii % 2)
                            dve.wait_ge(drained[b + 1], at(f"drained{b + 1}", half, "mergeA", i, ii // 2 + 1))
                            nc.vector.tensor_tensor(two(m[:, MU * i + ii, :]), cols[b], two(gate[:, ii % 2, :]),
                                                    ALU.mult).then_inc(drained[b], 1)

                dve.wait_ge(side_done, half + 1)
                for i in spans(dve, half, "conv"):
                    width = ext(half, T - 1, CONV_BUF) + 1 - CONV_BUF
                    for k in range(8):
                        ahead(half, "conv", i, k)
                        if k == 3:
                            dve.wait_ge(drained[0], at("drained0", half, "conv", i, 1))
                            for bank, c, first, n in PIECES[half]:
                                e0 = ext(half, first, CONV_BUF)
                                last = nc.vector.tensor_tensor(u[:, e0:e0 + n], ps[1][:, bank, c:c + n],
                                                               v[:, first:first + n], ALU.mult)
                            last.then_inc(drained[1], 1)
                            dve.wait_ge(drained[1], at("drained1", half, "conv", i, 1))
                            tap = [per_channel(V_W + KE * w + i) for w in range(TAPS)]
                            nc.vector.tensor_scalar(cv[:, 0, 0:width], u[:, 0:width], tap[0], None, ALU.mult) \
                                .then_inc(conv_step, 1)
                            for w in range(1, TAPS):
                                dve.wait_ge(conv_step, at("conv_step", half, "conv", i, w))
                                nc.vector.scalar_tensor_tensor(cv[:, w % 2, 0:width], u[:, w:w + width], tap[w],
                                                               cv[:, (w - 1) % 2, 0:width], ALU.mult, ALU.add) \
                                    .then_inc(conv_step, 1)
                        if k == 5:
                            dve.wait_ge(conv_step, at("conv_step", half, "conv", i, TAPS))
                            for bank, c, first, n in PIECES[half]:
                                e0 = ext(half, first, CONV_BUF) - CONV_BUF
                                last = nc.vector.tensor_tensor(q[:, first:first + n], ps[2][:, bank, c:c + n],
                                                               cv[:, (TAPS - 1) % 2, e0:e0 + n], ALU.mult)
                            last.then_inc(drained[2], 1)
                        if k == 7:
                            dve.wait_ge(zb_sigmoid, at("zb_sigmoid", half, "conv", i, 1))
                            nc.vector.tensor_tensor(two(zb_silu[:, :]), cols[3], two(zb_sig[:, :]), ALU.mult) \
                                .then_inc(drained[3], 1)
                            for b in (2, 3):
                                dve.wait_ge(drained[b], at(f"drained{b}", half, "conv", i, 1))
                            nc.vector.tensor_tensor(yrc[:, :], q[:, :], zb_silu[:, :], ALU.mult).then_inc(y_raw, 1)
                    y_lo(half, "conv", i, 1, i, yrc[:, :])

                def merged_split_lo(s):
                    dve.wait_ge(merged_hi, at("merged_hi", half, "split", s, 1))
                    if 2 * s >= KD:
                        dve.wait_ge(merged_split, at("merged_split", half, "split", min(2 * s - KD + 1, s - 1), 1))
                    nc.vector.tensor_tensor(ms[:, s, 1, :], m[:, s, :], f32(ms[:, s, 0, :]), ALU.subtract) \
                        .then_inc(merged_split, 1)

                for i in spans(dve, half, "mergeB", peel_last=True):
                    for k in range(3 * MU):
                        ahead(half, "mergeB", i, k)
                        if isinstance(i, int) and k in (3 * MU - 3, 3 * MU - 2):
                            n = EARLY // 2
                            s0 = 0 if k == 3 * MU - 3 else n
                            for s in range(s0, s0 + n):
                                merged_split_lo(s)
                        if k % 3 == 2:
                            ii = k // 3
                            b = 2 * (ii % 2)
                            dve.wait_ge(drained[b + 1], at(f"drained{b + 1}", half, "mergeB", i, ii // 2 + 1))
                            nc.vector.tensor_tensor(two(part[:, ii % 2, :]), cols[b], two(gate[:, ii % 2, :]),
                                                    ALU.mult).then_inc(drained[b], 1)
                            dve.wait_ge(drained[b], at(f"drained{b}", half, "mergeB", i, ii // 2 + 1))
                            mb = m[:, MU * i + ii, :]
                            nc.vector.tensor_tensor(mb, mb, part[:, ii % 2, :], ALU.add).then_inc(merged, 1)

                for s in range(EARLY, KD):
                    merged_split_lo(s)
                out = f"out{half}"

                def sum_block(i, e, t0=0, t1=TT, turned=None, summed=None, made=None, more=0):
                    eb = 2 * i + e
                    tf = min(t1, TT - 1)
                    short = t1 == TT
                    if turned is not None:
                        dve.wait_ge(turned, 1)
                    else:
                        dve.wait_ge(turned_back, at("turned_back", half, out, i, e + 1))
                    if half == 0:
                        dve.wait_ge(xr_landed[e], 16 * XR_DMAS * i + 16 * XR_DMAS)
                        a = xr[:, e, t0:tf, :], xr[0:TL, e, TT - 1, :]
                        g = fg[:, e, :]
                    else:
                        a = res[:, t0:tf, bass.ds(eb * P, P)], res[0:TL, TT - 1, bass.ds(eb * P, P)]
                        g = fin_g[:, bass.ds(eb * P, P)]
                    o = (flat[2 + e][:, t0 * P:tf * P].rearrange("p (t n) -> p t n", n=P),
                         flat[2 + e][0:TL, (TT - 1) * P:TT * P])
                    n0 = at("sum_step", half, out, i, 2 * e) + more
                    parts = range(1 + short)
                    for z in parts:
                        ins = nc.vector.tensor_tensor(a[z], a[z], o[z], ALU.add)
                    ins.then_inc(sum_step, 1)
                    dve.wait_ge(sum_step, n0 + 1)
                    for z in parts:
                        ins = nc.vector.tensor_tensor(o[z], a[z], a[z], ALU.mult)
                    ins.then_inc(sum_step, 1)
                    dve.wait_ge(sum_step, n0 + 2)
                    total = sums[:, eb, t0:tf], sums[0:TL, eb, TT - 1:TT]
                    for z in parts:
                        ins = nc.vector.reduce_sum(total[z], o[z], mybir.AxisListType.X)
                    ins.then_inc(drained[2 + e] if summed is None else summed, 1)

                    def times_g():
                        gs = g.rearrange("p (a n) -> p a n", a=1).broadcast_to([P, tf - t0, P]), g[0:TL]
                        for z in parts:
                            ins = nc.vector.tensor_tensor(a[z], a[z], gs[z], ALU.mult)
                        ins.then_inc(sum_made if made is None else made, 1)
                    return times_g

                def scale_xk(i, e):
                    dve.wait_ge(xk_landed[e], 16 * XK_DMAS * i + 16 * XK_DMAS)
                    a = xk[:, e, 0:TT - 1, :]
                    nc.vector.tensor_tensor(a, a, rstd1[:, 0:TT - 1].rearrange("p (t a) -> p t a", a=1)
                                            .broadcast_to([P, TT - 1, P]), ALU.mult)
                    a = xk[0:TL, e, TT - 1, :]
                    nc.vector.tensor_scalar(a, a, rstd1[0:TL, TT - 1:TT], None, ALU.mult).then_inc(xk_scaled, 1)

                def next_h_lo(i, e):
                    h_lo(2 * i + e, 2 + e, at("h_hi", 0, out, i, e + 1))

                if half == 0:
                    scale_xk(0, 0)
                for i in spans(dve, half, out, peel_first=True, peel_last=True):
                    first = isinstance(i, int) and i == 0
                    last_i = isinstance(i, int) and i > 0
                    for k in range(4):
                        if not (half == 1 and last_i):
                            ahead(half, out, i, k)
                        if k == 0 and first and half == 1:
                            dve.wait_ge(states_turned, 1)
                            nc.vector.tensor_copy(so[0:2 * HALO, :], flat[3][0:2 * HALO, 0:E]) \
                                .then_inc(drained[3], 1)
                        if k == 0 and not first:
                            sum_block(i - 1, 1)()
                        if k == 2 and first and half == 1:
                            dve.wait_ge(res_landed, 16 * (len(X_RUNS[1]) + 1))
                        if k == 2:
                            sum_block(i, 0)()
                        if half == 0 and k == 1:
                            next_h_lo(i, 0)
                            scale_xk(i, 1)
                        if half == 0 and k == 3:
                            next_h_lo(i, 1)
                            if not last_i:
                                scale_xk(i + 1, 0)
                i = PHASES[out][0] - 1
                t0 = 0
                if half == 1:
                    t0 = FT
                    times_g = sum_block(i, 1, 0, FT, first_tiles_turned, first_tiles_summed, first_tiles_made)
                    dve.wait_ge(drained[2], count["drained2"])
                    dve.wait_ge(first_tiles_summed, 1)
                    nc.vector.reduce_sum(ssqy[:, 0:FT], sums[:, :, 0:FT].rearrange("p e t -> p t e"),
                                         mybir.AxisListType.X).then_inc(first_tiles_norm, 1)
                    dve.wait_ge(first_tiles_norm, 1)
                    nc.vector.tensor_scalar(vary[:, 0:FT], ssqy[:, 0:FT], 1.0 / D, EPS, ALU.mult, ALU.add) \
                        .then_inc(first_tiles_norm, 1)
                    times_g()
                    dve.wait_ge(first_tiles_norm, 3)
                    dve.wait_ge(first_tiles_made, 1)
                    dve.wait_ge(sum_made, at("sum_made", half, out, i, 1))
                    for tt in range(FT):
                        nc.vector.tensor_scalar(res[:, tt, :], res[:, tt, :], rstdy[:, tt:tt + 1], None, ALU.mult) \
                            .then_inc(y_normed_dve, 1)
                times_g = sum_block(i, 1, t0, more=2 * half)
                for b in (2, 3):
                    dve.wait_ge(drained[b], count[f"drained{b}"] if half == 1 else base[f"drained{b}", 1, "pool"])
                nc.vector.reduce_sum(ssqy[:, t0:TT], sums[:, :, t0:TT].rearrange("p e t -> p t e"),
                                     mybir.AxisListType.X).then_inc(norm_step, 1)
                dve.wait_ge(norm_step, at("norm_step", half, "final", 0, 1))
                nc.vector.tensor_scalar(vary[:, t0:TT], ssqy[:, t0:TT], 1.0 / D, EPS, ALU.mult, ALU.add) \
                    .then_inc(norm_step, 1)
                times_g()
            dve.wait_ge(norm_step, at("norm_step", 1, "final", 0, 3))
            dve.wait_ge(sum_made, at("sum_made", 1, "out1", PHASES["out1"][0], 0))
            for tt in DVE_TILES[FT:]:
                r = rows_of(tt)
                nc.vector.tensor_scalar(res[0:r, tt, :], res[0:r, tt, :], rstdy[0:r, tt:tt + 1], None, ALU.mult) \
                    .then_inc(y_normed_dve, 1)


_INS = ['x_prompt', 'x_sample', 'state_pool', 'state_conv', 'norm_g', 'w_in', 'b_gate', 'w_pool_mix',
        'pool_scale', 'w_conv', 'w_proj_pool', 'w_proj_conv', 'w_out', 'final_norm_g']


def kernel(**inputs):
    import numpy as _np
    import concourse.bacc as _bacc
    from concourse import mybir as _mybir
    from concourse.bass_utils import run_bass_kernel_spmd as _run

    nc = _bacc.Bacc("TRN2", target_bir_lowering=False, num_devices=1)
    arrays, args = {}, []
    for name in _INS:
        a = _np.ascontiguousarray(inputs[name])
        arrays[f"in_{name}_dram"] = a
        args.append(nc.dram_tensor(f"in_{name}_dram", a.shape, _mybir.dt.from_np(a.dtype), kind="ExternalInput").ap())
    depth, _, pool_buf, e_pool = inputs['state_pool'].shape
    conv_buf, e_conv = inputs['state_conv'].shape[2:]
    b, db = inputs['x_prompt'].shape[0], inputs['x_sample'].shape[0]
    outs = [inputs['x_prompt'].shape, inputs['x_sample'].shape, (depth, b, pool_buf, e_pool),
            (depth, b, conv_buf, e_conv), (depth, db, pool_buf, e_pool), (depth, db, conv_buf, e_conv)]
    for i, shape in enumerate(outs):
        args.append(nc.dram_tensor(f"out_{i}_dram", tuple(shape), _mybir.dt.float32, kind="ExternalOutput").ap())
    bass_hybrid_stream_step(nc, *args)
    r = _run(nc, [arrays], core_ids=[0])
    return tuple(r.results[0][f"out_{i}_dram"] for i in range(len(outs)))
```
